# Optimizing a Trainium2 kernel written in Bass

```python
import jax, jax.numpy as jnp
from jax import lax
import numpy as np

D_MODEL = 1024
BATCH = 1
SEQ = 128
DEPTH = 2
DEC_BATCH = 1
DEC_SEQ = 512
PAST_LEN = 128

GRID_W = 64
HEAD_DIM = 64
GROUP_WIDTH = D_MODEL // 4
CONV_CH = GROUP_WIDTH
MLA_HEADS = GROUP_WIDTH // HEAD_DIM
MLA_NOPE = 64
MLA_ROPE = 32
MLA_V = GROUP_WIDTH // MLA_HEADS
MLA_Q_LORA = 192
MLA_KV_LORA = 128
GQA_HEADS = GROUP_WIDTH // HEAD_DIM
GQA_KV_HEADS = 2
SWA_HEADS = GROUP_WIDTH // HEAD_DIM
SWA_KV_HEADS = 2
WINDOW = 128
Q_BLOCK = 128
D_FF = 2816
ROPE_THETA = 10000.0
EPS = 1e-6
NEG_INF = -1e30
ATTN_SCALE = HEAD_DIM ** -0.5
MLA_SCALE = (MLA_NOPE + MLA_ROPE) ** -0.5
IN_SIZES = (3 * CONV_CH, MLA_Q_LORA, MLA_KV_LORA, MLA_ROPE, GQA_HEADS * HEAD_DIM,
            2 * GQA_KV_HEADS * HEAD_DIM, SWA_HEADS * HEAD_DIM, 2 * SWA_KV_HEADS * HEAD_DIM)
IN_COLS = sum(IN_SIZES)
IN_SPLITS = tuple(sum(IN_SIZES[:i + 1]) for i in range(len(IN_SIZES) - 1))

kernel_name = 'hybrid_parallel_group_diffusion_step'

def rmsnorm(x, g):
    xf = x.astype(jnp.float32)
    y = xf * lax.rsqrt(jnp.mean(xf * xf, axis=-1, keepdims=True) + EPS)
    return (y * g.astype(jnp.float32)).astype(x.dtype)

def conv3(x, w):
    xp = jnp.pad(x, ((0, 0), (1, 1), (0, 0)))
    return xp[:, :-2] * w[0] + xp[:, 1:-1] * w[1] + xp[:, 2:] * w[2]

def axial_tables(T, dim):
    rows = T // GRID_W
    row = jnp.repeat(jnp.arange(rows, dtype=jnp.float32), GRID_W)
    col = jnp.tile(jnp.arange(GRID_W, dtype=jnp.float32), rows)
    half = dim // 2
    inv = jnp.power(ROPE_THETA, -jnp.arange(0, half, 2, dtype=jnp.float32) / half)
    ar = row[:, None] * inv
    ac = col[:, None] * inv
    return (jnp.cos(ar)[:, None, :], jnp.sin(ar)[:, None, :], jnp.cos(ac)[:, None, :], jnp.sin(ac)[:, None, :])

def rope_half(x, c, s):
    x1, x2 = jnp.split(x, 2, axis=-1)
    return jnp.concatenate([x1 * c - x2 * s, x2 * c + x1 * s], axis=-1)

def axial_rope(x, tables):
    cr, sr, cc, sc = tables
    xr, xc = jnp.split(x.astype(jnp.float32), 2, axis=-1)
    return jnp.concatenate([rope_half(xr, cr, sr), rope_half(xc, cc, sc)], axis=-1).astype(x.dtype)

def group_heads(q, kvh):
    B, T, H, d = q.shape
    return q.reshape(B, T, kvh, H // kvh, d)

def blocked_attention(qs, ks, vs, scale, sink=None):
    B, T, KVH, G, _ = qs[0].shape
    nb = T // Q_BLOCK
    qb = tuple(jnp.moveaxis(q.reshape(B, nb, Q_BLOCK, *q.shape[2:]), 1, 0) for q in qs)
    sizes = [k.shape[1] for k in ks]

    def one(qblk):
        logits = [jnp.einsum('bqkgd,bskd->bkgqs', qi, ki).astype(jnp.float32) * scale for qi, ki in zip(qblk, ks)]
        if sink is not None:
            logits.append(jnp.broadcast_to(sink.reshape(KVH, G)[None, :, :, None, None].astype(jnp.float32),
                                           (B, KVH, G, Q_BLOCK, 1)))
        p = jax.nn.softmax(jnp.concatenate(logits, axis=-1), axis=-1)
        outs = []
        off = 0
        for vi, n in zip(vs, sizes):
            outs.append(jnp.einsum('bkgqs,bskd->bqkgd', p[..., off:off + n].astype(vi.dtype), vi))
            off += n
        return sum(outs[1:], outs[0])

    o = lax.map(one, qb)
    return jnp.moveaxis(o, 0, 1).reshape(B, T, -1)

def windowed_attention(q, k, v, q_ctx, k_ctx, v_ctx, sink, scale):
    B, T, KVH, G, Dh = q.shape
    nb = T // Q_BLOCK
    W3 = 3 * Q_BLOCK

    def band(a):
        ab = jnp.pad(a, ((0, 0), (Q_BLOCK, Q_BLOCK), (0, 0), (0, 0))).reshape(B, nb + 2, Q_BLOCK, KVH, a.shape[-1])
        return jnp.concatenate([ab[:, :-2], ab[:, 1:-1], ab[:, 2:]], axis=2)

    kw, vw = band(k), band(v)
    qb = q.reshape(B, nb, Q_BLOCK, KVH, G, Dh)
    qcb = q_ctx.reshape(B, nb, Q_BLOCK, KVH, G, Dh)
    qpos = jnp.arange(nb)[:, None, None] * Q_BLOCK + jnp.arange(Q_BLOCK)[None, :, None]
    kpos = jnp.arange(nb)[:, None, None] * Q_BLOCK - Q_BLOCK + jnp.arange(W3)[None, None, :]
    valid = (jnp.abs(kpos - qpos) <= WINDOW) & (kpos >= 0) & (kpos < T)
    s_loc = jnp.einsum('bnqkgd,bnskd->bnkgqs', qb, kw).astype(jnp.float32) * scale
    s_loc = jnp.where(valid[None, :, None, None], s_loc, NEG_INF)
    s_ctx = jnp.einsum('bnqkgd,bskd->bnkgqs', qcb, k_ctx).astype(jnp.float32) * scale
    s_sink = jnp.broadcast_to(sink.reshape(KVH, G)[None, None, :, :, None, None].astype(jnp.float32),
                              (B, nb, KVH, G, Q_BLOCK, 1))
    p = jax.nn.softmax(jnp.concatenate([s_loc, s_ctx, s_sink], axis=-1), axis=-1)
    L = k_ctx.shape[1]
    out = (jnp.einsum('bnkgqs,bnskd->bnqkgd', p[..., :W3].astype(vw.dtype), vw)
           + jnp.einsum('bnkgqs,bskd->bnqkgd', p[..., W3:W3 + L].astype(v_ctx.dtype), v_ctx))
    return out.reshape(B, T, KVH * G * Dh)

def mla_kv(ckv, kpe, w_kv_b):
    B, S, _ = ckv.shape
    kv = (ckv @ w_kv_b).reshape(B, S, MLA_HEADS, MLA_NOPE + MLA_V)
    k_nope, v = jnp.split(kv, [MLA_NOPE], axis=-1)
    k = jnp.concatenate([k_nope, jnp.broadcast_to(kpe, (B, S, MLA_HEADS, MLA_ROPE)).astype(k_nope.dtype)], axis=-1)
    return k, v

def layer(x, cond, lp, cache=None, ropes=None):
    B, T, _ = x.shape
    mod = (jax.nn.silu(cond) @ lp['w_ada'] + lp['b_ada'])[:, None, :]
    sh1, sc1, g1, sh2, sc2, g2 = jnp.split(mod, 6, axis=-1)
    h = rmsnorm(x, lp['norm1']) * (1 + sc1) + sh1
    proj = h @ lp['w_in']
    pa, pcq, pckv, pkpe, pq_c, pkv_c, pq_d, pkv_d = jnp.split(proj, IN_SPLITS, axis=-1)
    xa, gb, gc = jnp.split(pa, 3, axis=-1)
    y_a = gb * conv3(gc * xa, lp['conv_a'])
    cq = rmsnorm(pcq, lp['mla_q_norm'])
    q = (cq @ lp['mla_wq_b']).reshape(B, T, MLA_HEADS, MLA_NOPE + MLA_ROPE)
    q_nope, q_pe = jnp.split(q, [MLA_NOPE], axis=-1)
    ckv = rmsnorm(pckv, lp['mla_kv_norm'])
    kpe = pkpe[:, :, None, :]
    qc = rmsnorm(pq_c.reshape(B, T, GQA_HEADS, HEAD_DIM), lp['gqa_q_norm'])
    kc, vc = jnp.split(pkv_c.reshape(B, T, 2 * GQA_KV_HEADS, HEAD_DIM), 2, axis=2)
    kc = rmsnorm(kc, lp['gqa_k_norm'])
    qd = pq_d.reshape(B, T, SWA_HEADS, HEAD_DIM)
    kd, vd = jnp.split(pkv_d.reshape(B, T, 2 * SWA_KV_HEADS, HEAD_DIM), 2, axis=2)
    q_mla_raw = jnp.concatenate([q_nope, q_pe], axis=-1)[:, :, :, None, :]
    if cache is None:
        k_m, v_m = mla_kv(ckv, kpe, lp['mla_wkv_b'])
        y_b = blocked_attention((q_mla_raw,), (k_m,), (v_m,), MLA_SCALE)
        y_c = blocked_attention((group_heads(qc, GQA_KV_HEADS),), (kc,), (vc,), ATTN_SCALE)
        y_d = blocked_attention((group_heads(qd, SWA_KV_HEADS),), (kd,), (vd,), ATTN_SCALE, lp['swa_sink'])
        new = (ckv, pkpe, kc, vc, kd, vd)
    else:
        ckv_x, kpe_x, kc_x, vc_x, kd_x, vd_x = cache
        rope64, rope32 = ropes
        q_mla_rot = jnp.concatenate([q_nope, axial_rope(q_pe, rope32)], axis=-1)[:, :, :, None, :]
        k_l, v_l = mla_kv(ckv, axial_rope(kpe, rope32), lp['mla_wkv_b'])
        k_x, v_x = mla_kv(ckv_x, kpe_x[:, :, None, :], lp['mla_wkv_b'])
        y_b = blocked_attention((q_mla_rot, q_mla_raw), (k_l, k_x), (v_l, v_x), MLA_SCALE)
        y_c = blocked_attention((group_heads(axial_rope(qc, rope64), GQA_KV_HEADS), group_heads(qc, GQA_KV_HEADS)),
                                (axial_rope(kc, rope64), kc_x), (vc, vc_x), ATTN_SCALE)
        y_d = windowed_attention(group_heads(axial_rope(qd, rope64), SWA_KV_HEADS), axial_rope(kd, rope64), vd,
                                 group_heads(qd, SWA_KV_HEADS), kd_x, vd_x, lp['swa_sink'], ATTN_SCALE)
        new = None
    y = jnp.concatenate([y_a, y_b, y_c, y_d], axis=-1) @ lp['w_out']
    x = x + g1 * y
    h = rmsnorm(x, lp['norm2']) * (1 + sc2) + sh2
    u = conv3(h @ lp['w_up'], lp['conv_ff'])
    ua, ub = jnp.split(u, 2, axis=-1)
    x = x + g2 * ((jax.nn.silu(ua) * ub) @ lp['w_down'])
    return x, new

def setup_inputs(seed: int = 0) -> dict:
    key = jax.random.key(seed)
    ks = iter(jax.random.split(key, 32))
    nrm = lambda shape, s: jax.random.normal(next(ks), shape, jnp.float32) * s
    gain = lambda shape: 1.0 + nrm(shape, 0.05)
    L = DEPTH
    return {
        'x_prompt': nrm((BATCH, SEQ, D_MODEL), 1.0),
        'x_sample': nrm((DEC_BATCH, DEC_SEQ, D_MODEL), 1.0),
        'cache_mla_ckv': nrm((DEC_BATCH, L, PAST_LEN, MLA_KV_LORA), 1.0),
        'cache_mla_kpe': nrm((DEC_BATCH, L, PAST_LEN, MLA_ROPE), 1.0),
        'cache_gqa_k': nrm((DEC_BATCH, L, PAST_LEN, GQA_KV_HEADS, HEAD_DIM), 1.0),
        'cache_gqa_v': nrm((DEC_BATCH, L, PAST_LEN, GQA_KV_HEADS, HEAD_DIM), 1.0),
        'cache_swa_k': nrm((DEC_BATCH, L, PAST_LEN, SWA_KV_HEADS, HEAD_DIM), 1.0),
        'cache_swa_v': nrm((DEC_BATCH, L, PAST_LEN, SWA_KV_HEADS, HEAD_DIM), 1.0),
        'c': nrm((DEC_BATCH, D_MODEL), 1.0),
        'c_ctx': nrm((D_MODEL,), 1.0),
        'w_ada': nrm((L, D_MODEL, 6 * D_MODEL), D_MODEL ** -0.5),
        'b_ada': nrm((L, 6 * D_MODEL), 0.01),
        'norm1': gain((L, D_MODEL)),
        'w_in': nrm((L, D_MODEL, IN_COLS), D_MODEL ** -0.5),
        'conv_a': nrm((L, 3, CONV_CH), 0.5),
        'mla_q_norm': gain((L, MLA_Q_LORA)),
        'mla_wq_b': nrm((L, MLA_Q_LORA, MLA_HEADS * (MLA_NOPE + MLA_ROPE)), MLA_Q_LORA ** -0.5),
        'mla_kv_norm': gain((L, MLA_KV_LORA)),
        'mla_wkv_b': nrm((L, MLA_KV_LORA, MLA_HEADS * (MLA_NOPE + MLA_V)), MLA_KV_LORA ** -0.5),
        'gqa_q_norm': gain((L, HEAD_DIM)),
        'gqa_k_norm': gain((L, HEAD_DIM)),
        'swa_sink': nrm((L, SWA_HEADS), 0.5),
        'w_out': nrm((L, D_MODEL, D_MODEL), D_MODEL ** -0.5),
        'norm2': gain((L, D_MODEL)),
        'w_up': nrm((L, D_MODEL, 2 * D_FF), D_MODEL ** -0.5),
        'conv_ff': nrm((L, 3, 2 * D_FF), 0.5),
        'w_down': nrm((L, D_FF, D_MODEL), D_FF ** -0.5),
        'final_norm': gain((D_MODEL,)),
    }

def reference(x_prompt, x_sample, cache_mla_ckv, cache_mla_kpe, cache_gqa_k, cache_gqa_v, cache_swa_k, cache_swa_v,
              c, c_ctx, w_ada, b_ada, norm1, w_in, conv_a, mla_q_norm, mla_wq_b, mla_kv_norm, mla_wkv_b,
              gqa_q_norm, gqa_k_norm, swa_sink, w_out, norm2, w_up, conv_ff, w_down, final_norm):
    T_lat = x_sample.shape[1]
    ropes = (axial_tables(T_lat, HEAD_DIM), axial_tables(T_lat, MLA_ROPE))
    xp, xs = x_prompt, x_sample
    states = []
    for l in range(DEPTH):
        lp = {'w_ada': w_ada[l], 'b_ada': b_ada[l], 'norm1': norm1[l], 'w_in': w_in[l], 'conv_a': conv_a[l],
              'mla_q_norm': mla_q_norm[l], 'mla_wq_b': mla_wq_b[l], 'mla_kv_norm': mla_kv_norm[l],
              'mla_wkv_b': mla_wkv_b[l], 'gqa_q_norm': gqa_q_norm[l], 'gqa_k_norm': gqa_k_norm[l],
              'swa_sink': swa_sink[l], 'w_out': w_out[l], 'norm2': norm2[l], 'w_up': w_up[l],
              'conv_ff': conv_ff[l], 'w_down': w_down[l]}
        xp, st = layer(xp, c_ctx[None, :], lp)
        states.append(st)
        cache_l = (cache_mla_ckv[:, l], cache_mla_kpe[:, l], cache_gqa_k[:, l], cache_gqa_v[:, l],
                   cache_swa_k[:, l], cache_swa_v[:, l])
        xs, _ = layer(xs, c, lp, cache_l, ropes)
    new_mla_ckv, new_mla_kpe, new_gqa_k, new_gqa_v, new_swa_k, new_swa_v = [
        jnp.stack([s[i] for s in states], axis=1) for i in range(6)]
    y_prompt = rmsnorm(xp, final_norm)
    y_sample = rmsnorm(xs, final_norm)
    return (y_prompt, y_sample, new_mla_ckv, new_mla_kpe, new_gqa_k, new_gqa_v, new_swa_k, new_swa_v)


_drawn_inputs = setup_inputs


def setup_inputs(seed=0):
    import zlib

    import numpy as np

    out = dict(_drawn_inputs(seed))
    spreads = {}
    factors = {'cache_mla_ckv': 4.413,
     'cache_mla_kpe': 7.913,
     'cache_gqa_k': 5.497,
     'cache_gqa_v': 4.827,
     'mla_q_norm': 8.0,
     'gqa_q_norm': 8.0,
     'swa_sink': 64.0}
    for name, (base, spread) in spreads.items():
        noise = np.random.default_rng([zlib.crc32(name.encode()), seed]).standard_normal(out[name].shape)
        drawn = base * np.exp(spread * noise) if base else spread * noise
        out[name] = __import__('jax').numpy.asarray(drawn.astype(out[name].dtype))
    for name, factor in factors.items():
        out[name] = (out[name] * factor).astype(out[name].dtype)
    return out
```

```python
from contextlib import ExitStack

import numpy as np

import concourse.bass as bass
from concourse import mybir

F32 = mybir.dt.float32
F32R = mybir.dt.float32r
ACT = mybir.ActivationFunctionType
ALU = mybir.AluOpType
AXX = mybir.AxisListType.X

P = 128
D = 1024
DEPTH = 2
KT = D // P
NLAT, NCTX = 512, 128
QT = NLAT // P
CTX0 = NLAT + 2
T = CTX0 + NCTX + 2
HALF = T // 2
TILE0 = [P * i for i in range(QT)] + [CTX0]
TT = QT + 1
HD = 64
GRID_W = 64
FF = 2816
FT = FF // P
PAIRS = FT // 2
EPS = 1e-6
NEG = -1e30
SCALES = [HD ** -0.5, HD ** -0.5, 96 ** -0.5]
YTILE = [4, 6, 2]
QLORA, KVLORA, ROPE = 192, 128, 32
KEYS = P + NLAT + P
C_PAST, C_LAT, C_CTX = 0, P, P + NLAT
NADA = 24
ADA_A = 8

TOKEN_CHUNKS = [(1120, 256), (1376, 256), (768, 352), (1632, 256), (1888, 256)]
FEAT_CHUNKS = [512, 0, 256]
NPROJ = 2 * (len(TOKEN_CHUNKS) + len(FEAT_CHUNKS))
NOUT = 8
NFF = 6 * PAIRS
NW = NPROJ + NOUT + NFF
NRAW = 2 * NADA + NW
RAW, SPL = 3, 2
RMAX = 4 * 352

K_ID, K_MASK, K_ONE, K_SEL = 0, 128, 384, 512
K_C64, K_S64, K_C32, K_S32 = 514, 770, 1026, 1154
K_MH, K_N = 1282, 1322
HALFK = (P + NLAT) // 2


def raw_of_split(s):
    return 2 * ADA_A + s if s < NPROJ else 2 * NADA + s


def raw_of_ada(a):
    return a if a < 2 * ADA_A else NPROJ + a


RAW_KIND = {}
for _s in range(NW):
    RAW_KIND[raw_of_split(_s)] = ("w", _s)
for _a in range(2 * NADA):
    RAW_KIND[raw_of_ada(_a)] = ("ada", _a)
assert sorted(RAW_KIND) == list(range(NRAW)) and NRAW % RAW == 0 and NW % SPL == 0


HEADS = 12
NQ = TT
NKV = 8
PAST = TT
NVEC = 23


def kv_of(h):
    return h - 4 if h >= 8 else 2 * (h // 4) + (h % 4) // 2


def window(h, q):
    return (max(q - 1, 0), min(q + 2, QT)) if h // 4 == 1 else (0, QT)


def queries(h, k):
    if k == 0 or h // 4 != 1:
        return 0, QT
    return max(k - 2, 0), min(k + 1, QT)


def prob_col(h, q, k):
    return 0 if k == 0 or q == QT else P * (k - window(h, q)[0])


P_SEQ = [TT] + list(range(TT))


def attention_order():
    order = []

    def probs(h):
        out = []
        for n, k in enumerate(P_SEQ):
            out.append([("T", ("P", h, k))] + ([("V", h, P_SEQ[n - 1])] if n else []))
        out.append([("V", h, P_SEQ[-1])])
        return out
    ch = ADA_A
    for h in range(HEADS):
        group = h % 4 == 0
        p = probs(h - 1) if h else []
        if group:
            for e in p:
                order += e
            p = []
        if h == 8:
            for i in range(TT + 2):
                if i < TT + 1:
                    order.append(("T", ("MT", i)))
                if 1 <= i:
                    if i <= TT:
                        order.append(("T", ("MQ", i - 1)))
                    order.append(("T", ("MV", i - 1)))
            order.append(("PREP", 2))
        if h == 0 or kv_of(h) != kv_of(h - 1):
            order += [("T", ("K", kv_of(h), 0)), ("T", ("K", kv_of(h), 1))]
        order += [("T", ("Q", h, 0)), ("T", ("Q", h, 1))]
        if h == 3:
            order.append(("PREP", 1))
        todo = [ch] + ([ch + 1] if h % 3 == 0 else [])
        ch += len(todo)
        order.append(("ADA", todo[0]))
        s = [[("S", h, q)] for q in range(NQ)]
        order += s[0]
        order.append(("MOVE", todo[0]))
        order += s[1]
        s = s[2:]
        first = True
        while s or p:
            for e in p[:2 if len(p) > len(s) else 1] + s[:1]:
                order += e
            p, s = p[2 if len(p) > len(s) else 1:], s[1:]
            if first:
                order.append(("SEL", todo[0]))
                if len(todo) > 1:
                    order.append(("ADA", todo[1]))
                first = False
        if len(todo) > 1:
            order += [("MOVE", todo[1]), ("SEL", todo[1])]
        if h == HEADS - 1:
            for e in probs(h):
                order += e
    assert ch == NADA
    return order


ORDER = attention_order()
FILLS = [e[1] for e in ORDER if e[0] == "T"]
FILL_AT = {key: n for n, key in enumerate(FILLS)}
assert len(FILLS) == len(FILL_AT)
NFILL = len(FILLS)
NEV = [(NFILL + 1) // 2, NFILL // 2]
NS_ = NQ * HEADS
SIDX = {e[1:]: n for n, e in enumerate(x for x in ORDER if x[0] == "S")}
assert all(SIDX[(h, q)] == NQ * h + q for h in range(HEADS) for q in range(NQ))


class Chain:

    def __init__(self, eng, sem, base):
        self.eng, self.sem, self.base, self.n = eng, sem, base, 0

    def then(self, ins):
        ins.then_inc(self.sem, 1)
        self.n += 1

    def wait(self):
        self.eng.wait_ge(self.sem, self.base + self.n)


DVE_OWN = 28


def backbone_program(nc, x_prompt, x_sample, cache_mla_ckv, cache_mla_kpe, cache_gqa_k, cache_gqa_v,
                     cache_swa_k, cache_swa_v, c, c_ctx, w_ada, b_ada, norm1, w_in, conv_a, mla_q_norm,
                     mla_wq_b, mla_kv_norm, mla_wkv_b, gqa_q_norm, gqa_k_norm, swa_sink, w_out, norm2,
                     w_up, conv_ff, w_down, final_norm, consts,
                     y_prompt, y_sample, new_ckv, new_kpe, new_gk, new_gv, new_sk, new_sv):
    ctx = ExitStack()
    with ctx:
        def sb(name, shape, dt=F32, stack=ctx):
            return stack.enter_context(nc.sbuf_tensor(name, shape, dt))

        def sem(name):
            return ctx.enter_context(nc.semaphore(name))

        X = sb("X", [P, KT, T])
        H_hi = sb("H_hi", [P, KT, T], F32R)
        H_lo = sb("H_lo", [P, KT, T], F32R)
        RW = sb("RW", [P, RAW, RMAX])
        W_hi = sb("W_hi", [P, SPL, RMAX], F32R)
        W_lo = sb("W_lo", [P, SPL, RMAX], F32R)
        K = sb("K", [P, K_N])
        VT = sb("VT", [P, 72 + 132])
        MOD = sb("MOD", [P, 48, 2])
        AB = sb("AB", [P, 2, KT, 2])
        CT = sb("CT", [P, KT, 32])
        R = sb("R", [P, 256])
        NS = sb("NS", [P, 2, 8])
        FN = sb("FN", [P, KT])
        SS = sb("SS", [P, 2, 40])
        ST = sb("ST", [P, 4, 4])
        SK = sb("SK", [P, 4])
        SE = sb("SE", [P, 4])
        IDENT = K[:, K_ID:K_ID + P]
        ONES = K[:, K_ONE:K_ONE + P]
        SINK = sb("SINK", [P, 4])
        GAIN = sb("GAIN", [P, 6 * HD + KVLORA])
        CX = sb("CX", [P, 160 + 4 * P])
        WQ = sb("WQ", [96, 2, 384])
        WK = sb("WK", [P, 512])

        b = ExitStack()
        PR = sb("PR", [P, 2, QT * (P + NLAT) + P], F32, b)
        PT = sb("PT", [P, 2, NLAT], F32, b)
        QTR = sb("QTR", [P, 2, NQ * P], F32, b)
        b.close()
        b = ExitStack()
        SQ = sb("SQ", [P, 2, T], F32, b)
        SUM = sb("SUM", [P, T], F32, b)
        XN = sb("XN", [P, 2, T], F32, b)
        HF = sb("HF", [P, 2, T], F32, b)
        DG = sb("DG", [P, TT, P], F32, b)
        U = sb("U", [P, 2, 2, T + 2], F32, b)
        b.close()
        b = ExitStack()
        GC = sb("GC", [P, 2, T], F32, b)
        TP = sb("TP", [P, 2, T + 2], F32, b)
        CV = sb("CV", [P, 2, T], F32, b)
        HS = sb("HS", [P, TT, 384], F32, b)
        VR = sb("VR", [70, P], F32, b)
        VF = sb("VF", [66, 2, P], F32, b)
        VQ = sb("VQ", [2, 96], F32, b)
        sb("rest", [P, 1560 - 96], F32, b)

        a = ExitStack()
        PMG = sb("PMG", [P, TT, 512], F32, a)
        PMS = sb("PMS", [P, TT, 512], F32, a)
        PMM = sb("PMM", [P, TT, 352], F32, a)
        QS = sb("QS", [P, TT, 4, P], F32, a)
        KS = sb("KS", [P, TT + 1, 4, P], F32, a)
        KTR = sb("KTR", [P, 2, KEYS], F32, a)
        t = ExitStack()
        TA = sb("TA", [P, 2, 4 * HD], F32, t)
        TB = sb("TB", [P, 2, 4 * HD], F32, t)
        t.close()
        t = ExitStack()
        CQ = sb("CQ", [P, 2, 3, P], F32, t)
        t.close()
        a.close()
        a = ExitStack()
        CF = sb("CF", [P, 2, 2, T], F32, a)
        G_hi = sb("G_hi", [P, 2, 2, T], F32R, a)
        G_lo = sb("G_lo", [P, 2, 2, T], F32R, a)
        DN = sb("DN", [P, KT, T], F32, a)
        a.close()
        a = ExitStack()
        XIN = sb("XIN", [P, TT, D], F32, a)
        CR = sb("CR", [16, P], F32, a)
        FR = sb("FR", [KT, P], F32, a)
        YO = sb("YO", [P, KT, T], F32, a)
        OUT = sb("OUT", [P, 2, D], F32, a)
        a.close()
        b.close()

        PS = ctx.enter_context(nc.psum_tensor("PS", [P, 8, 512], F32))

        const_in, x_in, c_in, f_in = sem("const_in"), sem("x_in"), sem("c_in"), sem("f_in")
        vec_in = sem("vec_in")
        raw_in = [sem(f"raw_in{i}") for i in range(RAW)]
        setup_v, x_tr, x_ev = sem("setup_v"), sem("x_tr"), sem("x_ev")
        c_tr, c_silu, f_tr, f_ev = sem("c_tr"), sem("c_silu"), sem("f_tr"), sem("f_ev")
        v_tr, v_ev = sem("v_tr"), sem("v_ev")
        ada_mm, ada_ev, ada_sel, mod_ok = sem("ada_mm"), sem("ada_ev"), sem("ada_sel"), sem("mod_ok")
        w_hi, w_lo, w_used = sem("w_hi"), sem("w_lo"), sem("w_used")
        sq_done, ss_add, st_mm, nv, rv, dg, bc_mm = (sem(n) for n in (
            "sq_done", "ss_add", "st_mm", "nv", "rv", "dg", "bc_mm"))
        xn, hf, h_hi, h_lo = sem("xn"), sem("hf"), sem("h_hi"), sem("h_lo")
        pj_ev, feat, gated, ya_hi, ya_lo = (sem(n) for n in ("pj_ev", "feat", "gated", "ya_hi", "ya_lo"))
        hn, hp, head_in, zeroed = sem("hn"), sem("hp"), sem("head_in"), sem("zeroed")
        raw_q, raw_k, rot_q, rot_k, rot_own, wq_ok = (sem(n) for n in (
            "raw_q", "raw_k", "rot_q", "rot_k", "rot_own", "wq_ok"))
        tr_mm = sem("tr_mm")
        tr_ev = [sem("tr_ev_act"), sem("tr_ev_dve")]
        s_mm, s_max, s_nb, s_exp, s_sink, s_den, s_rec, s_norm = (sem(n) for n in (
            "s_mm", "s_max", "s_nb", "s_exp", "s_sink", "s_den", "s_rec", "s_norm"))
        pv_mm, y_hi, y_lo = sem("pv_mm"), sem("y_hi"), sem("y_lo")
        new_out, o_ev, x_mid, x_fin = sem("new_out"), sem("o_ev"), sem("x_mid"), sem("x_fin")
        up_ev, cv_own, cv_done, silu_ok, g_f, g_hi, g_lo = (sem(n) for n in (
            "up_ev", "cv_own", "cv_done", "silu_ok", "g_f", "g_hi", "g_lo"))
        dn_add, dve_own = sem("dn_add"), sem("dve_own")
        fin_y, fin_tr, fin_ev = sem("fin_y"), sem("fin_tr"), sem("fin_ev")
        y_out = [sem("y_out0"), sem("y_out1")]

        block = ctx.enter_context(nc.Block())

        def v_ap(g, kv, tile):
            if g == 2:
                return PMG[:, kv, 384:384 + HD] if tile == PAST else PMS[:, tile, HD * kv:HD * (kv + 1)]
            if tile == PAST:
                return CX[:, 288 + 256 * g + HD * kv:288 + 256 * g + HD * (kv + 1)]
            return (PMG, PMS)[g][:, tile, 384 + HD * kv:384 + HD * (kv + 1)]

        def score_ap(h, q, n):
            if q == QT:
                return PS[:, 2 * (n % 2), 0:P]
            if h // 4 == 1:
                lo, hi = window(h, q)
                return PS[:, 2 * (n % 2), 0:P * (1 + hi - lo)]
            return PS[:, 2 * (n % 2):2 * (n % 2) + 2, 0:HALFK]

        def prob_ap(h, q):
            c0 = q * (P + NLAT)
            if q == QT:
                return PR[:, h % 2, c0:c0 + P]
            if h // 4 == 1:
                lo, hi = window(h, q)
                return PR[:, h % 2, c0:c0 + P * (1 + hi - lo)]
            return PR[:, h % 2, c0:c0 + P + NLAT].rearrange("p (b n) -> p b n", n=HALFK)

        def y_cols(k):
            return (CTX0, CTX0 + P) if k == TT else (0, NLAT)

        def evac_fill(eng, copy, l, key):
            n = FILL_AT[key]
            bank = PS[:, 4 + n % 2, :]
            eng.wait_ge(tr_mm, l * NFILL + (n + 1))
            done = tr_ev[n % 2]
            kind = key[0]
            if kind == "P":
                _, h, k = key
                i = 6 * h + P_SEQ.index(k)
                if i >= 2:
                    eng.wait_ge(pv_mm, l * 6 * HEADS + i - 1)
                c0, c1 = (0, P) if k == TT else (P * queries(h, k)[0], P * queries(h, k)[1])
                copy(PT[:, i % 2, c0:c1], bank[:, c0:c1]).then_inc(done, 1)
            elif kind == "Q":
                _, h, part = key
                if h >= 2:
                    eng.wait_ge(s_mm, l * NS_ + NQ * (h - 1))
                c0, c1 = (0, NLAT) if part == 0 else (NLAT, NLAT + P)
                copy(QTR[:, h % 2, c0:c1], bank[:, 0:c1 - c0]).then_inc(done, 1)
            elif kind == "K":
                _, kv, part = key
                if kv >= 2:
                    last = max(h for h in range(HEADS) if kv_of(h) == kv - 2)
                    eng.wait_ge(s_mm, l * NS_ + NQ * (last + 1))
                c0, c1 = (0, 512) if part == 0 else (512, KEYS)
                copy(KTR[:, kv % 2, c0:c1], bank[:, 0:c1 - c0]).then_inc(done, 1)
            elif kind == "MT":
                i = key[1]
                if i >= 2:
                    eng.wait_ge(tr_mm, l * NFILL + (FILL_AT[("MV", i - 2)] + 1))
                else:
                    eng.wait_ge(rot_q, l * 3 + 2)
                if i < TT:
                    copy(CQ[0:96, i % 2, 0:2, :], bank[0:96, 0:2 * P].rearrange("p (k n) -> p k n", n=P))
                copy(CQ[:, i % 2, 2, :], bank[:, 2 * P:3 * P]).then_inc(done, 1)
            elif kind == "MQ":
                eng.wait_ge(new_out, l * 96 + 96)
                copy(PMG[:, key[1], 0:384], bank[:, 0:384]).then_inc(done, 1)
            else:
                src = bank.rearrange("p (h n) -> p h n", n=P)
                copy(KS[:, key[1], :, 0:HD], src[:, :, 0:HD])
                eng.wait_ge(new_out, l * 96 + 96)
                eng.wait_ge(raw_q, l * 3 + 2)
                i = key[1]
                dst = PMG[:, 0:4, 384:384 + HD] if i == PAST else \
                    PMS[:, i, 0:4 * HD].rearrange("p (h n) -> p h n", n=HD)
                copy(dst, src[:, :, HD:P]).then_inc(done, 1)

        def rope(eng, wait, done, dst, src, table_c, table_s, heads, dim):
            q4, w = dim // 4, heads * dim

            def by_head(ap):
                return ap.rearrange("p (h n) -> p h n", h=heads)

            def spread(c0, n):
                return K[:, c0:c0 + n].rearrange("p (o n) -> p o n", o=1).to_broadcast([P, heads, n])
            for t0 in range(0, QT, 2):
                for t in (t0, t0 + 1):
                    eng.tensor_tensor(by_head(TA[:, t - t0, 0:w]), src(t), spread(table_c + dim * t, dim), ALU.mult)
                    for r in range(4):
                        o, i = q4 * r, q4 * (r ^ 1)
                        ins = eng.tensor_tensor(by_head(TB[:, t - t0, 0:w])[:, :, o:o + q4], src(t)[:, :, i:i + q4],
                                                spread(table_s + dim * t + o, q4), ALU.mult)
                done(ins)
                wait()
                for t in (t0, t0 + 1):
                    ins = eng.tensor_tensor(dst(t), by_head(TA[:, t - t0, 0:w]), by_head(TB[:, t - t0, 0:w]), ALU.add)
                if t0 + 2 < QT:
                    done(ins)
                    wait()
            return ins

        def rope_queries(eng, sync, l, g):
            sync.wait_ge(tr_mm, l * NFILL + (FILL_AT[("Q", 4 * g - 1, 1)] + 1))
            if g == 1:
                sync.wait_ge(rot_q, l * 3 + 1)
                src, dst, dim = (lambda t: PMS[:, t, 0:256].rearrange("p (h n) -> p h n", n=HD)), \
                    (lambda t: QS[:, t, :, 0:HD]), HD
            else:
                sync.wait_ge(tr_mm, l * NFILL + (FILL_AT[("MV", TT)] + 1))
                for b in range(2):
                    last = max(n for n in range(NFILL) if n % 2 == b and FILLS[n][0] == "MQ")
                    sync.wait_ge(tr_ev[b], l * NEV[b] + (last // 2 + 1))
                src, dst, dim = (lambda t: PMG[:, t, 0:384].rearrange("p (h n) -> p h n", n=96)[:, :, HD:96]), \
                    (lambda t: QS[:, t, :, HD:96]), ROPE
            tc, ts = (K_C64, K_S64) if dim == HD else (K_C32, K_S32)
            own = Chain(sync, rot_own, l * 6 + 3 * (g - 1))
            rope(eng, own.wait, own.then, dst, src, tc, ts, 4, dim).then_inc(rot_q, 1)

        @block.sync
        def _(sp):
            sp.dma_start(K[:, :], consts).then_inc(const_in, 16)
            for i in range(TT):
                src = x_sample[0, P * i:P * (i + 1), :] if i < QT else x_prompt[0, :, :]
                sp.dma_start(XIN[:, i, :], src).then_inc(x_in, 16)
            sp.dma_start(CR[0:8, :], c.rearrange("a (k p) -> (a k) p", p=P)).then_inc(c_in, 16)
            sp.dma_start(CR[8:16, :], c_ctx.rearrange("(k p) -> k p", p=P)).then_inc(c_in, 16)
            sp.dma_start(FR[:, :], final_norm.rearrange("(k p) -> k p", p=P)).then_inc(f_in, 16)

            def load_raw(l, r, src):
                dst = RW[:, r % RAW, 0:src.shape[1] * src.shape[2]]
                sp.dma_start(dst.rearrange("p (k n) -> p k n", n=src.shape[2]), src).then_inc(raw_in[r % RAW], 16)

            def slot_free(l, r):
                kind, n = RAW_KIND[r - RAW] if r >= RAW else ("w", r - RAW)
                if kind == "ada":
                    value = l * (2 * NADA) + (n + 1)
                else:
                    value = l * NW + (RAW + n + 1)
                sp.wait_ge(ada_mm if kind == "ada" else w_lo, value)

            def up_src(l, j, s):
                v = w_up[bass.ds(l, 1), :, bass.ds(j * P + s * FF, P)]
                return v.rearrange("a (k p) n -> p (a k) n", p=P)

            def down_src(l, i, q):
                v = w_down[bass.ds(l, 1), bass.ds(i * (2 * P), 2 * P), 512 * q:512 * (q + 1)]
                return v.rearrange("a (k p) n -> p (a k) n", p=P)

            with sp.Fori(0, DEPTH) as l:
                sp.wait_ge(o_ev, l * NOUT + 1)
                sp.wait_ge(x_mid, l * KT + 1)

                def small(dst, src):
                    sp.dma_start(dst, src).then_inc(vec_in, 16)

                def row(v, p=P):
                    return v[bass.ds(l, 1), :].rearrange("a (k p) -> (a k) p", p=p)
                small(VR[0:48, :], row(b_ada))
                small(VR[48:56, :], row(norm1))
                small(VR[56:64, :], row(norm2))
                small(VR[64:70, :], conv_a[bass.ds(l, 1), :, :].rearrange("a t (k p) -> (a t k) p", p=P))
                small(VQ[:, :], row(mla_q_norm, 96))
                cf = conv_ff.rearrange("l t (k p) -> l (t k) p", p=P)
                for s in range(2):
                    small(VF[:, s, :], cf[bass.ds(l, 1), 66 * s:66 * (s + 1), :].rearrange("a r p -> (a r) p"))
                small(SINK[:, :], swa_sink[bass.ds(l, 1), :].to_broadcast([P, 4]))
                for j in range(6):
                    g = gqa_q_norm if j < 4 else gqa_k_norm
                    small(GAIN[:, HD * j:HD * (j + 1)], g[bass.ds(l, 1), :].to_broadcast([P, HD]))
                small(GAIN[:, 6 * HD:], mla_kv_norm[bass.ds(l, 1), :].to_broadcast([P, KVLORA]))
                small(CX[:, 0:128], cache_mla_ckv[0, bass.ds(l, 1), :, :].rearrange("a t n -> (a t) n"))
                small(CX[:, 128:160], cache_mla_kpe[0, bass.ds(l, 1), :, :].rearrange("a t n -> (a t) n"))
                for j, v in enumerate((cache_gqa_k, cache_gqa_v, cache_swa_k, cache_swa_v)):
                    small(CX[:, 160 + P * j:160 + P * (j + 1)],
                          v[0, bass.ds(l, 1), :, :, :].rearrange("a t h n -> (a t) (h n)"))
                small(WQ[:, :, :], mla_wq_b[bass.ds(l, 1), :, :].rearrange("a (k p) n -> p (a k) n", p=96))
                small(WK[:, :], mla_wkv_b[bass.ds(l, 1), :, :].rearrange("a p n -> (a p) n"))
                for r in range(2 * NADA + NPROJ + NOUT):
                    kind, n = RAW_KIND[r]
                    ch, kh = divmod(n, 2)
                    if kind == "ada":
                        src = w_ada[bass.ds(l, 1), 512 * kh:512 * (kh + 1), 256 * ch:256 * (ch + 1)]
                    elif n < NPROJ:
                        c0, w = (TOKEN_CHUNKS + [(c_, 256) for c_ in FEAT_CHUNKS])[ch]
                        src = w_in[bass.ds(l, 1), 512 * kh:512 * (kh + 1), c0:c0 + w]
                    else:
                        ch, kh = ch - NPROJ // 2, 1 - kh
                        src = w_out[bass.ds(l, 1), 512 * kh:512 * (kh + 1), 256 * ch:256 * (ch + 1)]
                    src = src.rearrange("a (k p) n -> p (a k) n", p=P)
                    if kind == "w" and n in (12, NPROJ + 1):
                        flat = (w_in if n == 12 else w_out).rearrange("l r n -> (l r) n")
                        src = flat[bass.ds(l * D, D // 2), 0:2 * P].rearrange("(k p) n -> p k n", p=P)
                    slot_free(l, r)
                    load_raw(l, r, src)
                    if r == 2 * ADA_A + NPROJ + 3:
                        sp.wait_ge(head_in, l + 1)
                        for dst, src in (
                                (new_ckv, PMM[:, QT, QLORA:QLORA + KVLORA]),
                                (new_kpe, PMM[:, QT, QLORA + KVLORA:]),
                                (new_gk, PMG[:, QT, 256:384]), (new_gv, PMG[:, QT, 384:512]),
                                (new_sk, PMS[:, QT, 256:384]), (new_sv, PMS[:, QT, 384:512])):
                            d = dst[0, bass.ds(l, 1)]
                            d = d.rearrange("a t n -> (a t) n") if len(d.shape) == 3 else \
                                d.rearrange("a t h n -> (a t) (h n)")
                            sp.dma_start(d, src).then_inc(new_out, 16)
                base = 2 * NADA + NPROJ + NOUT
                for e in range(4):
                    src = up_src(l, e // 2, e % 2)
                    slot_free(l, base + e)
                    load_raw(l, base + e, src)
                with sp.Fori(1, PAIRS) as i:
                    for e in range(6):
                        src = up_src(l, i * 2 + e // 2, e % 2) if e < 4 else down_src(l, i - 1, e - 4)
                        sp.wait_ge(w_lo, l * NW + i * 6 + (3 + NPROJ + NOUT + 4 - 6 + e - RAW + 1))
                        load_raw(l, base + 4 + e, src)
                for q in range(2):
                    src = down_src(l, PAIRS - 1, q)
                    slot_free(l, NRAW - 2 + q)
                    load_raw(l, NRAW - 2 + q, src)
            sp.wait_ge(new_out, 96 * DEPTH)
            for i in range(TT):
                sp.wait_ge(fin_ev, 2 * i + 2)
                dst = y_sample[0, P * i:P * (i + 1), :] if i < QT else y_prompt[0, :, :]
                sp.dma_start(dst, OUT[:, i % 2, :]).then_inc(y_out[i % 2], 16)
            sp.wait_ge(y_out[0], 48)
            sp.wait_ge(y_out[1], 32)

        @block.gpsimd
        def _(pool):
            pool.sem_inc(w_lo, RAW)
            pool.sem_inc(w_used, SPL)
            pool.sem_inc(o_ev, 1)
            pool.sem_inc(x_mid, 1)
            pool.sem_inc(dn_add, 8)
            pool.wait_ge(const_in, 16)

            def low(value, slot, raw, width):
                pool.wait_ge(w_hi, value)
                nc.gpsimd.tensor_tensor(W_lo[:, slot, 0:width], RW[:, raw, 0:width],
                                        W_hi[:, slot, 0:width].bitcast(F32), ALU.subtract).then_inc(w_lo, 1)

            def item(l, s):
                low(l * NW + (s + 1), s % SPL, raw_of_split(s) % RAW, RMAX if s in (4, 5) else 1024)

            def norm_root(N):
                pool.wait_ge(nv, N + 1)
                nc.gpsimd.tensor_tensor(NS[:, 1, 0:TT], NS[:, 0, 0:TT], K[:, K_MH:K_MH + TT],
                                        ALU.pow).then_inc(rv, 1)

            with pool.Fori(0, DEPTH) as l:
                norm_root(l * 2)
                for s in range(10):
                    item(l, s)
                pool.wait_ge(hn, l + 1)
                nc.gpsimd.tensor_tensor(SS[:, 1, 0:40], SS[:, 0, 0:40], K[:, K_MH:K_MH + 40],
                                        ALU.pow).then_inc(hp, 1)
                for s in range(10, NPROJ):
                    item(l, s)
                for g in (1, 2):
                    rope_queries(nc.gpsimd, pool, l, g)
                for s in range(NPROJ, NPROJ + NOUT + 2):
                    item(l, s)
                norm_root(l * 2 + 1)
                s0 = NPROJ + NOUT + 2
                for s in range(s0, s0 + 4):
                    item(l, s)
                with pool.Fori(0, PAIRS - 1) as i:
                    for e in range(6):
                        s = s0 + 4 + e
                        low(l * NW + i * 6 + (s + 1), s % SPL, raw_of_split(s) % RAW, 1024)
            norm_root(2 * DEPTH)

        @block.scalar
        def _(act):
            def copy(dst, src):
                return nc.scalar.activation(dst, src, ACT.Copy)

            act.wait_ge(setup_v, 3)
            act.wait_ge(c_tr, 1)
            nc.scalar.activation(CT[:, :, 0:2], PS[:, 6, 0:16].rearrange("p (m k) -> p k m", m=2),
                                 ACT.Silu).then_inc(c_silu, 1)

            def split_hi(slot, raw, landed, used, width):
                act.wait_ge(raw_in[raw], landed)
                act.wait_ge(w_used, used)
                copy(W_hi[:, slot, 0:width], RW[:, raw, 0:width]).then_inc(w_hi, 1)

            def item(l, s):
                r = raw_of_split(s)
                split_hi(s % SPL, r % RAW, l * (16 * NRAW // RAW) + 16 * (r // RAW + 1),
                         l * NW + (s + 1), RMAX if s in (4, 5) else 1024)

            def squares(N, ready):
                for t in range(KT):
                    ready(t)
                    if t >= 2:
                        act.wait_ge(ss_add, N * 7 + max(t - 2, 1))
                    nc.scalar.activation(SQ[:, t % 2, :], X[:, t, :], ACT.Square).then_inc(sq_done, 1)

            def modulate(N, w, t):
                act.wait_ge(xn, N * KT + (t + 1))
                if t >= 2:
                    act.wait_ge(h_lo, N * KT + (t - 1))
                for cond, (c0, c1) in enumerate(((0, NLAT), (CTX0, CTX0 + NCTX))):
                    nc.scalar.activation(HF[:, t % 2, c0:c1], XN[:, t % 2, c0:c1], ACT.Identity,
                                         bias=MOD[:, 24 * w + t, cond:cond + 1],
                                         scale=AB[:, w, t, cond:cond + 1]).then_inc(hf, 1)
                act.wait_ge(hf, N * (2 * KT) + (2 * t + 2))
                copy(H_hi[:, t, :], HF[:, t % 2, :]).then_inc(h_hi, 1)

            def ada_move(l, ch, bank):
                act.wait_ge(ada_mm, l * (2 * NADA) + (2 * ch + 2))
                if ch > 0:
                    act.wait_ge(ada_sel, l * NADA + ch)
                copy(R[:, :], PS[:, bank, 0:256]).then_inc(ada_ev, 1)

            with act.Fori(0, DEPTH) as l:
                act.wait_ge(x_fin, l * KT + 1)
                squares(l * 2, lambda t: act.wait_ge(x_fin, l * KT + (t + 1)))
                act.wait_ge(v_tr, l + 1)
                copy(VT[:, 0:70], PS[:, 3, 0:70])
                copy(VT[0:96, 70:72], PS[0:96, 3, 70:72])
                copy(VT[:, 72:204], PS[:, 3, 72:204]).then_inc(v_ev, 1)
                for ch in range(ADA_A):
                    ada_move(l, ch, ch % 2)
                item(l, 0)
                item(l, 1)
                act.wait_ge(mod_ok, l * 4 + 2)
                for t in range(KT):
                    modulate(l * 2, 0, t)

                for ch in range(len(TOKEN_CHUNKS)):
                    item(l, 2 * ch + 2)
                    act.wait_ge(w_used, l * NW + (SPL + 2 * ch + 2))
                    dst, c0, w = ((PMG, 0, 256), (PMG, 256, 256), (PMM, 0, 352), (PMS, 0, 256),
                                  (PMS, 256, 256))[ch]
                    for i in range(TT):
                        copy(dst[:, i, c0:c0 + w], PS[:, (TT * ch + i) % 8, 0:w]).then_inc(pj_ev, 1)
                    item(l, 2 * ch + 3)
                item(l, 12)
                act.wait_ge(w_used, l * NW + (SPL + 12))
                for o in range(2):
                    copy(GC[:, o, :].rearrange("p (h n) -> p h n", h=2),
                         PS[:, 2 + 2 * o:4 + 2 * o, 0:HALF]).then_inc(feat, 1)
                item(l, 13)
                item(l, 14)
                item(l, 15)

                act.wait_ge(head_in, l + 1)
                act.wait_ge(zeroed, l * 3 + 3)
                for g, pm in enumerate((PMG, PMS)):
                    copy(KS[:, QT, 2 * g:2 * g + 2, 0:HD], pm[:, QT, 256:384].rearrange("p (h n) -> p h n", n=HD))
                    o = 160 + 2 * P * g
                    ins = copy(KS[:, PAST, 2 * g:2 * g + 2, HD:P],
                               CX[:, o:o + P].rearrange("p (h n) -> p h n", n=HD))
                ins.then_inc(raw_k, 1)

                def raw_queries(g):
                    if g < 2:
                        if g == 1:
                            act.wait_ge(tr_mm, l * NFILL + (FILL_AT[("Q", 3, 1)] + 1))
                        for t in range(TT):
                            src = (PMG, PMS)[g][:, t, 0:256].rearrange("p (h n) -> p h n", n=HD)
                            ins = copy(QS[:, t, :, HD:P] if t < QT else QS[:, t, :, 0:HD], src)
                        ins.then_inc(raw_q, 1)
                        return
                    last = max(n for n in range(1, NFILL, 2) if FILLS[n][0] == "MQ")
                    act.wait_ge(tr_ev[1], l * NEV[1] + (last // 2 + 1))
                    last = max(n for n in range(0, NFILL, 2) if FILLS[n][0] == "MQ")
                    act.wait_ge(tr_ev[0], l * NEV[0] + (last // 2 + 1))
                    for t in range(TT):
                        src = PMG[:, t, 0:384].rearrange("p (h n) -> p h n", n=96)
                        copy(QS[:, t, :, 0:HD], src[:, :, 0:HD])
                        ins = copy(QS[:, t, :, 96:P] if t < QT else QS[:, t, :, HD:96], src[:, :, HD:96])
                    ins.then_inc(raw_q, 1)
                    kpe = PMM[:, QT, 320:352].rearrange("p (o n) -> p o n", o=1).to_broadcast([P, 4, ROPE])
                    copy(KS[:, QT, :, HD:96], kpe)
                    kpe = CX[:, 128:160].rearrange("p (o n) -> p o n", o=1).to_broadcast([P, 4, ROPE])
                    copy(KS[:, PAST, :, 96:P], kpe).then_inc(raw_k, 1)
                raw_queries(0)

                for o in range(2):
                    act.wait_ge(gated, l * 2 + (o + 1))
                    copy(H_hi[:, o, :], CV[:, o, :]).then_inc(ya_hi, 1)
                act.wait_ge(ya_lo, l * 2 + 2)

                def exponentials(h, q):
                    g, j = divmod(h, 4)
                    n = SIDX[(h, q)]
                    act.wait_ge(s_nb, l * NS_ + (n + 1))
                    if q == 0 and h >= 2:
                        act.wait_ge(tr_mm, l * NFILL + (FILL_AT[("P", h - 2, QT)] + 1))
                    nb = ST[:, 1, n % 4:n % 4 + 1]
                    if g == 1:
                        nc.scalar.activation(SE[:, n % 4:n % 4 + 1], SINK[:, j:j + 1], ACT.Exp,
                                             bias=nb).then_inc(s_sink, 1)
                    nc.scalar.activation(prob_ap(h, q), score_ap(h, q, n), ACT.Exp, bias=nb, scale=SCALES[g],
                                         accum_out=ST[:, 2, n % 4:n % 4 + 1]).then_inc(s_exp, 1)

                waiting = None
                for e in ORDER:
                    if e[0] == "S":
                        if waiting:
                            exponentials(*waiting)
                        waiting = e[1:]
                        continue
                    if e[0] == "T" and e[1][0] == "P" and waiting and waiting[0] == e[1][1]:
                        exponentials(*waiting)
                        waiting = None
                    if e[0] == "T" and FILL_AT[e[1]] % 2 == 0:
                        evac_fill(act, copy, l, e[1])
                    elif e[0] == "PREP":
                        if e[1] == 2:
                            act.wait_ge(tr_mm, l * NFILL + (FILL_AT[("K", 3, 1)] + 1))
                        raw_queries(e[1])
                    elif e[0] == "MOVE":
                        ada_move(l, e[1], 7)
                    elif e == ("V", HEADS - 1, 0):
                        item(l, NPROJ)
                        item(l, NPROJ + 1)
                    elif e[0] == "V" and e[2] in (TT, QT):
                        h, k = e[1:]
                        i, r0, (c0, c1) = 6 * h + P_SEQ.index(k), HD * (h % 2), y_cols(k)
                        act.wait_ge(pv_mm, l * 6 * HEADS + (i + 1))
                        copy(H_hi[r0:r0 + HD, YTILE[h // 4] + h % 4 // 2, c0:c1],
                             PS[r0:r0 + HD, 6, 0:c1 - c0]).then_inc(y_hi, 1)
                    if waiting:
                        exponentials(*waiting)
                        waiting = None

                act.wait_ge(new_out, l * 96 + 96)
                for ch in range(NOUT // 2):
                    item(l, NPROJ + 2 * ch + 2)
                    act.wait_ge(w_used, l * NW + (SPL + NPROJ + 2 * ch + 2))
                    for o in range(2):
                        b0 = 4 * (ch % 2) + 2 * o
                        copy(DN[:, 2 * ch + o, :].rearrange("p (h n) -> p h n", h=2),
                             PS[:, b0:b0 + 2, 0:HALF]).then_inc(o_ev, 1)
                    item(l, NPROJ + 2 * ch + 3)
                squares(l * 2 + 1, lambda t: act.wait_ge(x_mid, l * KT + (t + 2)))
                for t in range(KT):
                    modulate(l * 2 + 1, 1, t)

                def up_out(i, ch, used, first):
                    act.wait_ge(w_used, used)
                    for s in range(2):
                        if not first:
                            act.wait_ge(cv_done, l * 44 + i * 4 + (2 * ch + s + 1 - 4))
                        b0 = 4 * ch + 2 * s
                        copy(U[:, ch, s, 1:T + 1].rearrange("p (h n) -> p h n", h=2),
                             PS[:, b0:b0 + 2, 0:HALF]).then_inc(up_ev, 1)

                def silu(i, ch):
                    act.wait_ge(cv_done, l * 44 + i * 4 + (2 * ch + 2))
                    nc.scalar.activation(CF[:, ch, 0, :], CF[:, ch, 0, :], ACT.Silu).then_inc(silu_ok, 1)

                def g_high(i, ch, slot):
                    act.wait_ge(g_f, l * 22 + i * 2 + (ch + 1))
                    copy(G_hi[:, slot, ch, :], CF[:, ch, 1, :]).then_inc(g_hi, 1)

                s0 = NPROJ + NOUT
                item(l, s0 + 2)
                up_out(0, 0, l * NW + (SPL + s0 + 2), True)
                item(l, s0 + 3)
                silu(0, 0)
                item(l, s0 + 4)
                up_out(0, 1, l * NW + (SPL + s0 + 4), True)
                item(l, s0 + 5)
                g_high(0, 0, 0)
                silu(0, 1)
                g_high(0, 1, 0)
                s0 += 4
                with act.Fori(0, PAIRS // 2) as m:
                    for b_ in range(2):
                        i = m * 2 + (1 + b_)

                        def item_i(e, b_=b_):
                            s = s0 + 6 * b_ + e
                            r = raw_of_split(s)
                            split_hi(s % SPL, r % RAW, l * (16 * NRAW // RAW) + m * 64 + 16 * (r // RAW + 1),
                                     l * NW + m * 12 + (s + 1), 1024)

                        def used_i(e, b_=b_):
                            return l * NW + m * 12 + (SPL + s0 + 6 * b_ + e + 1)
                        item_i(2)
                        up_out(i, 0, used_i(1), False)
                        item_i(3)
                        silu(i, 0)
                        item_i(4)
                        up_out(i, 1, used_i(3), False)
                        item_i(5)
                        g_high(i, 0, (1 + b_) % 2)
                        item_i(6)
                        silu(i, 1)
                        item_i(7)
                        g_high(i, 1, (1 + b_) % 2)

            squares(2 * DEPTH, lambda t: act.wait_ge(x_fin, DEPTH * KT + t + 1))
            for t in range(KT):
                act.wait_ge(xn, 2 * DEPTH * KT + t + 1)
                for c0, c1 in ((0, NLAT), (CTX0, CTX0 + NCTX)):
                    ins = nc.scalar.activation(YO[:, t, c0:c1], XN[:, t % 2, c0:c1], ACT.Copy,
                                               scale=FN[:, t:t + 1])
                ins.then_inc(fin_y, 1)
            for n in range(2 * TT):
                act.wait_ge(fin_tr, n + 1)
                if n >= 4:
                    act.wait_ge(y_out[n // 2 % 2], 16 * (n // 4))
                copy(OUT[:, n // 2 % 2, 512 * (n % 2):512 * (n % 2 + 1)], PS[:, n % 4, :]).then_inc(fin_ev, 1)

        @block.tensor
        def _(pe):
            def mm(out, lhsT, rhs, start, stop):
                return nc.tensor.matmul(out, lhsT, rhs, start=start, stop=stop, skip_group_check=True)

            def tr(out, in_):
                n = in_.shape[0]
                return nc.tensor.transpose(out, in_, K[0:n, K_ID:K_ID + n])

            pe.wait_ge(const_in, 16)
            for i in range(TT):
                pe.wait_ge(x_in, 80)
                for hb in range(2):
                    n = 2 * i + hb
                    if n >= 6:
                        pe.wait_ge(x_ev, n - 5)
                    for t in range(4):
                        ins = tr(PS[:, n % 6, P * t:P * (t + 1)], XIN[:, i, P * (4 * hb + t):P * (4 * hb + t + 1)])
                    ins.then_inc(x_tr, 1)
            pe.wait_ge(c_in, 32)
            tr(PS[:, 6, 0:16], CR[:, :]).then_inc(c_tr, 1)
            pe.wait_ge(f_in, 16)
            tr(PS[:, 7, 0:KT], FR[:, :]).then_inc(f_tr, 1)
            pe.wait_ge(c_silu, 1)
            pe.wait_ge(f_ev, 1)
            pe.wait_ge(x_fin, KT)

            def ada_half(l, ch, kh, bank):
                a = 2 * ch + kh
                r = raw_of_ada(a)
                pe.wait_ge(raw_in[r % RAW], l * (16 * NRAW // RAW) + 16 * (r // RAW + 1))
                for kk in range(4):
                    ins = mm(PS[32 * kk:32 * kk + 32, bank, 0:256], CT[:, 4 * kh + kk, :],
                             RW[:, r % RAW, 256 * kk:256 * (kk + 1)], kh == 0, kh == 1)
                ins.then_inc(ada_mm, 1)

            def select(l, ch, bank, col):
                pe.wait_ge(ada_ev, l * NADA + (ch + 1))
                for o in range(2):
                    ins = mm(PS[:, bank, col + 2 * o:col + 2 * o + 2], R[:, P * o:P * (o + 1)],
                             K[:, K_SEL:K_SEL + 2], True, True)
                ins.then_inc(ada_sel, 1)

            def statistics(N):
                pe.wait_ge(ss_add, N * 7 + 7)
                for i in range(TT):
                    ins = mm(PS[:, 5, i:i + 1], SUM[:, TILE0[i]:TILE0[i] + P], ONES[:, 0:1], True, True)
                ins.then_inc(st_mm, 1)
                for i in range(TT):
                    pe.wait_ge(dg, N * TT + (i + 1))
                    out = PS[:, 6, P * i:P * (i + 1)] if i < QT else PS[:, 7, 0:P]
                    ins = mm(out, ONES, DG[:, i, :], True, True)
                ins.then_inc(bc_mm, 1)

            def three(outs, w, cols, moving, first, last):
                mhi, mlo = moving
                for stat, mov, st, sp_ in ((W_hi, mhi, first, False), (W_hi, mlo, False, False),
                                           (W_lo, mhi, False, last)):
                    for hf_, out in enumerate(outs):
                        ins = mm(out, stat[:, w, cols:cols + P], mov[:, HALF * hf_:HALF * (hf_ + 1)], st, sp_)
                return ins

            def halves(pair):
                return [PS[:, 2 * pair + b_, 0:HALF] for b_ in range(2)]

            with pe.Fori(0, DEPTH) as l:
                pe.wait_ge(dn_add, l * (8 * PAIRS) + 8)
                pe.wait_ge(vec_in, l * (16 * NVEC) + 16 * NVEC)
                tr(PS[:, 3, 0:70], VR[:, :])
                tr(PS[0:96, 3, 70:72], VQ[:, :])
                tr(PS[:, 3, 72:138], VF[:, 0, :])
                tr(PS[:, 3, 138:204], VF[:, 1, :]).then_inc(v_tr, 1)
                for ch in range(ADA_A):
                    if ch >= 2:
                        pe.wait_ge(ada_ev, l * NADA + (ch - 1))
                    ada_half(l, ch, 0, ch % 2)
                    ada_half(l, ch, 1, ch % 2)
                    if ch:
                        select(l, ch - 1, 2, 4 * (ch - 1))
                    if ch == 3:
                        statistics(l * 2)
                select(l, ADA_A - 1, 2, 4 * (ADA_A - 1))

                def w_ready(s):
                    pe.wait_ge(w_lo, l * NW + (RAW + s + 1))

                for ch, (_, w) in enumerate(TOKEN_CHUNKS):
                    for kh in range(2):
                        s = 2 * ch + kh
                        w_ready(s)
                        for kk in range(4):
                            k = 4 * kh + kk
                            if ch == 0:
                                pe.wait_ge(h_lo, l * (2 * KT) + (k + 1))
                            for i in range(TT):
                                idx = TT * ch + i
                                if k == 0 and idx >= 8:
                                    pe.wait_ge(pj_ev, l * 25 + (idx - 7))
                                out = PS[:, idx % 8, 0:w]
                                c0 = TILE0[i]
                                whi = W_hi[:, s % SPL, w * kk:w * (kk + 1)]
                                wlo = W_lo[:, s % SPL, w * kk:w * (kk + 1)]
                                mm(out, H_hi[:, k, c0:c0 + P], whi, k == 0, False)
                                mm(out, H_hi[:, k, c0:c0 + P], wlo, False, False)
                                ins = mm(out, H_lo[:, k, c0:c0 + P], whi, False, k == KT - 1)
                        ins.then_inc(w_used, 1)
                for f in range(3):
                    for kh in range(2):
                        s = 2 * len(TOKEN_CHUNKS) + 2 * f + kh
                        w_ready(s)
                        if kh == 0:
                            pe.wait_ge(pj_ev, l * 25 + (22 if f == 0 else 25))
                            if f == 2:
                                pe.wait_ge(feat, l * 2 + 2)
                        for kk in range(4):
                            for o in range(2):
                                pair = (1 + o, (3 + o) % 4, 1 + o)[f]
                                ins = three(halves(pair), s % SPL, 2 * P * kk + P * o,
                                            (H_hi[:, 4 * kh + kk, :], H_lo[:, 4 * kh + kk, :]),
                                            kh == 0 and kk == 0, kh == 1 and kk == 3)
                        ins.then_inc(w_used, 1)

                pe.wait_ge(gated, l * 2 + 2)
                for e in ORDER:
                    if e[0] == "T":
                        key = e[1]
                        n = FILL_AT[key]
                        bank = PS[:, 4 + n % 2, :]
                        if n >= 2:
                            pe.wait_ge(tr_ev[n % 2], l * NEV[n % 2] + n // 2)
                        if key[0] == "K":
                            _, kv, part = key
                            g = min(kv // 2, 2)
                            if part == 0 and kv in (0, 4):
                                pe.wait_ge(raw_k, l * 2 + (1 if kv == 0 else 2))
                                pe.wait_ge(rot_k, l * 2 + (1 if kv == 0 else 2))
                                if kv == 0:
                                    pe.wait_ge(zeroed, l * 3 + 3)
                            for x, tile in enumerate((PAST, 0, 1, 2) if part == 0 else (3, 4)):
                                ins = tr(bank[:, P * x:P * (x + 1)], KS[:, tile, kv if kv < 4 else kv - 4, :])
                        elif key[0] == "Q":
                            _, h, part = key
                            if h % 4 == 0 and part == 0:
                                pe.wait_ge(raw_q, l * 3 + (h // 4 + 1))
                                pe.wait_ge(rot_q, l * 3 + (h // 4 + 1))
                            for x, tile in enumerate(range(QT) if part == 0 else (QT,)):
                                ins = tr(bank[:, P * x:P * (x + 1)], QS[:, tile, h % 4, :])
                        elif key[0] == "P":
                            _, h, k = key
                            if k == TT:
                                pe.wait_ge(s_norm, l * NS_ + NQ * (h + 1))
                                ins = tr(bank[:, 0:P], prob_ap(h, QT))
                            else:
                                q0, q1 = queries(h, k)
                                for q in range(q0, q1):
                                    c0 = q * (P + NLAT) + prob_col(h, q, k)
                                    ins = tr(bank[:, P * q:P * (q + 1)], PR[:, h % 2, c0:c0 + P])
                        elif key[0] == "MT":
                            i = key[1]
                            if i < TT:
                                tr(bank[0:96, 0:P], PMM[:, i, 0:96])
                                tr(bank[0:96, P:2 * P], PMM[:, i, 96:192])
                            ins = tr(bank[:, 2 * P:3 * P],
                                     PMM[:, i, 192:320] if i < TT else CX[:, 0:128])
                        elif key[0] == "MQ":
                            i = key[1]
                            m_ = FILL_AT[("MT", i)]
                            pe.wait_ge(tr_ev[m_ % 2], l * NEV[m_ % 2] + (m_ // 2 + 1))
                            pe.wait_ge(wq_ok, l + 1)
                            for k in range(2):
                                ins = mm(bank[:, 0:384], CQ[0:96, i % 2, k, :], WQ[:, k, :], k == 0, k == 1)
                        else:
                            i = key[1]
                            m_ = FILL_AT[("MT", i)]
                            pe.wait_ge(tr_ev[m_ % 2], l * NEV[m_ % 2] + (m_ // 2 + 1))
                            ins = mm(bank, CQ[:, i % 2, 2, :], WK[:, :], True, True)
                        ins.then_inc(tr_mm, 1)
                    elif e[0] == "S":
                        h, q = e[1:]
                        n, kv = SIDX[(h, q)], kv_of(h)
                        if n >= 2:
                            pe.wait_ge(s_exp, l * NS_ + (n - 1))
                        if q in (0, 1):
                            due = [("Q", h, 0), ("Q", h, 1), ("K", kv, 0), ("K", kv, 1)] if q == 0 else []
                            for key in due:
                                m_ = FILL_AT[key]
                                pe.wait_ge(tr_ev[m_ % 2], l * NEV[m_ % 2] + (m_ // 2 + 1))
                        b0 = 2 * (n % 2)
                        qt = QTR[:, h % 2, P * q:P * (q + 1)]
                        kt = KTR[:, kv % 2, :]
                        if q == QT:
                            ins = mm(PS[:, b0, 0:P], qt, kt[:, C_CTX:C_CTX + P], True, True)
                        elif h // 4 == 1:
                            lo, hi = window(h, q)
                            mm(PS[:, b0, 0:P], qt, kt[:, 0:P], True, True)
                            ins = mm(PS[:, b0, P:P * (1 + hi - lo)], qt,
                                     kt[:, C_LAT + P * lo:C_LAT + P * hi], True, False)
                            if q >= 1:
                                ins = mm(PS[:, b0, P:2 * P], IDENT, K[:, K_MASK:K_MASK + P], False, False)
                            if q <= QT - 2:
                                c0 = P * (hi - lo)
                                ins = mm(PS[:, b0, c0:c0 + P], IDENT, K[:, K_MASK + P:K_MASK + 2 * P],
                                         False, True)
                        else:
                            for b_ in range(2):
                                ins = mm(PS[:, b0 + b_, 0:HALFK], qt, kt[:, HALFK * b_:HALFK * (b_ + 1)],
                                         True, True)
                        ins.then_inc(s_mm, 1)
                    elif e[0] == "V":
                        h, k = e[1:]
                        i, r0 = 6 * h + P_SEQ.index(k), HD * (h % 2)
                        m_ = FILL_AT[("P", h, k)]
                        pe.wait_ge(tr_ev[m_ % 2], l * NEV[m_ % 2] + (m_ // 2 + 1))
                        yi = 2 * h + (k != TT)
                        if k in (TT, 0) and yi:
                            pe.wait_ge(y_lo, l * (2 * HEADS) + yi)
                        kv = kv_of(h) - 4 if h >= 8 else kv_of(h) % 2
                        tile = {TT: QT, 0: PAST}.get(k, k - 1)
                        c0, c1 = (0, P) if k == TT else (P * queries(h, k)[0], P * queries(h, k)[1])
                        if h == 8 and k == TT:
                            for m_ in (FILL_AT[("MV", TT)], FILL_AT[("MV", TT - 1)], FILL_AT[("MV", TT - 2)]):
                                pe.wait_ge(tr_ev[m_ % 2], l * NEV[m_ % 2] + (m_ // 2 + 1))
                        mm(PS[r0:r0 + HD, 6, c0:c1], v_ap(h // 4, kv, tile), PT[:, i % 2, c0:c1],
                           k in (TT, 0), k in (TT, QT)).then_inc(pv_mm, 1)
                    elif e[0] == "ADA":
                        pe.wait_ge(ada_ev, l * NADA + e[1])
                        ada_half(l, e[1], 0, 7)
                        ada_half(l, e[1], 1, 7)
                    elif e[0] == "SEL":
                        select(l, e[1], 7, 256 + 4 * (e[1] - ADA_A))

                for ch in range(NOUT // 2):
                    for x in range(2):
                        s = NPROJ + 2 * ch + x
                        w_ready(s)
                        if x == 0:
                            if ch == 0:
                                pe.wait_ge(s_exp, l * NS_ + NS_)
                            elif ch == 1:
                                for b_ in range(2):
                                    pe.wait_ge(tr_ev[b_], l * NEV[b_] + NEV[b_])
                                pe.wait_ge(y_lo, l * (2 * HEADS) + 2 * HEADS)
                                pe.wait_ge(mod_ok, l * 4 + 4)
                            else:
                                pe.wait_ge(o_ev, l * NOUT + (1 + 2 * (ch - 1)))
                        if ch == 0:
                            pe.wait_ge(y_lo, l * (2 * HEADS) + (16 if x == 0 else 2 * HEADS))
                            pe.wait_ge(ya_lo, l * 2 + 2)
                        for kk in range(4):
                            k = 4 * (1 - x) + kk
                            for o in range(2):
                                ins = three(halves(2 * (ch % 2) + o), s % SPL, 2 * P * kk + P * o,
                                            (H_hi[:, k, :], H_lo[:, k, :]), x == 0 and kk == 0,
                                            x == 1 and kk == 3)
                        ins.then_inc(w_used, 1)
                pe.wait_ge(o_ev, l * NOUT + (1 + NOUT))
                statistics(l * 2 + 1)

                def up_item(e, slot, ready, free, first):
                    pe.wait_ge(w_lo, ready)
                    free(e)
                    for k in range(KT):
                        if first and e == 0:
                            pe.wait_ge(h_lo, l * (2 * KT) + (KT + k + 1))
                        ins = three(halves(e), slot, P * k, (H_hi[:, k, :], H_lo[:, k, :]), k == 0, k == KT - 1)
                    ins.then_inc(w_used, 1)

                def down_item(q, slot, gslot, ready, free):
                    pe.wait_ge(w_lo, ready)
                    for t in range(4):
                        free(t)
                        for kc in range(2):
                            ins = three(halves(t), slot, 512 * kc + P * t,
                                        (G_hi[:, gslot, kc, :], G_lo[:, gslot, kc, :]), kc == 0, kc == 1)
                    ins.then_inc(w_used, 1)

                s0 = NPROJ + NOUT
                for e in range(4):
                    up_item(e, (s0 + e) % SPL, l * NW + (RAW + s0 + e + 1), lambda p: None, True)
                s0 += 4
                with pe.Fori(0, PAIRS // 2) as m:
                    for b_ in range(2):
                        i = m * 2 + (1 + b_)

                        def up_free(p):
                            pe.wait_ge(up_ev, l * 44 + i * 4 + (p + 1 - 4))
                            pe.wait_ge(dn_add, l * (8 * PAIRS) + i * 8 + (8 + 5 + p - 16))

                        def ready_i(e, b_=b_):
                            return l * NW + m * 12 + (RAW + s0 + 6 * b_ + e + 1)
                        for e in range(4):
                            up_item(e, (s0 + e) % SPL, ready_i(e), up_free, False)
                        pe.wait_ge(g_lo, l * 22 + i * 2)
                        down_item(0, s0 % SPL, b_ % 2, ready_i(4),
                                  lambda t: pe.wait_ge(up_ev, l * 44 + i * 4 + (t + 1)))
                        down_item(1, (s0 + 1) % SPL, b_ % 2, ready_i(5),
                                  lambda t: pe.wait_ge(dn_add, l * (8 * PAIRS) + i * 8 + (t + 1)))
                pe.wait_ge(g_lo, l * 22 + 22)
                for q in range(2):
                    s = NW - 2 + q
                    down_item(q, s % SPL, (PAIRS - 1) % 2, l * NW + (RAW + s + 1),
                              lambda t: pe.wait_ge(dn_add, l * (8 * PAIRS) + (8 + 8 * (PAIRS - 1) - 4 + 4 * q + t + 1)))

            pe.wait_ge(dn_add, 8 * PAIRS * DEPTH + 8)
            statistics(2 * DEPTH)
            pe.wait_ge(fin_y, KT)
            for n in range(2 * TT):
                if n >= 4:
                    pe.wait_ge(fin_ev, n - 3)
                c0 = TILE0[n // 2]
                for t in range(4):
                    ins = tr(PS[:, n % 4, P * t:P * (t + 1)], YO[:, 4 * (n % 2) + t, c0:c0 + P])
                ins.then_inc(fin_tr, 1)

        @block.vector
        def _(dve):
            v = nc.vector

            def copy(dst, src):
                return v.tensor_copy(dst, src)

            dve.wait_ge(const_in, 16)
            v.memset(CT[:, :, :], 0.0).then_inc(setup_v, 1)
            v.memset(X[:, :, NLAT:CTX0], 0.0).then_inc(setup_v, 1)
            v.memset(X[:, :, T - 2:T], 0.0).then_inc(setup_v, 1)
            for n in range(2 * TT):
                dve.wait_ge(x_tr, n + 1)
                c0, hb = TILE0[n // 2], n % 2
                ins = copy(X[:, 4 * hb:4 * hb + 4, c0:c0 + P], PS[:, n % 6, :].rearrange("p (t n) -> p t n", n=P))
                if n < 2 * TT - 1:
                    ins.then_inc(x_ev, 1)
                else:
                    ins.then_inc(x_fin, KT)
            dve.wait_ge(f_tr, 1)
            copy(FN[:, :], PS[:, 7, 0:KT]).then_inc(f_ev, 1)

            def norm_start(N):
                v.memset(HF[:, :, NLAT:CTX0], 0.0)
                v.memset(HF[:, :, T - 2:T], 0.0)
                for t in range(1, KT):
                    dve.wait_ge(sq_done, N * KT + (t + 1))
                    if t == 1:
                        v.tensor_tensor(SUM[:, :], SQ[:, 0, :], SQ[:, 1, :], ALU.add).then_inc(ss_add, 1)
                    else:
                        dve.wait_ge(ss_add, N * 7 + (t - 1))
                        v.tensor_tensor(SUM[:, :], SUM[:, :], SQ[:, t % 2, :], ALU.add).then_inc(ss_add, 1)
                dve.wait_ge(st_mm, N + 1)
                v.tensor_scalar(NS[:, 0, 0:TT], PS[:, 5, 0:TT], 1.0 / D, EPS, ALU.mult, ALU.add).then_inc(nv, 1)
                dve.wait_ge(rv, N + 1)
                for i in range(TT):
                    v.tensor_scalar(DG[:, i, :], IDENT, NS[:, 1, i:i + 1], None, ALU.mult).then_inc(dg, 1)
                for t in range(2):
                    normalise(N, t)

            def normalise(N, t):
                if t < 2:
                    dve.wait_ge(bc_mm, N + 1)
                elif isinstance(N, int):
                    dve.wait_ge(fin_y, t - 1)
                else:
                    dve.wait_ge(hf, N * (2 * KT) + (2 * t - 2))
                v.tensor_tensor(XN[:, t % 2, 0:NLAT], X[:, t, 0:NLAT], PS[:, 6, :], ALU.mult)
                v.tensor_tensor(XN[:, t % 2, CTX0:CTX0 + P], X[:, t, CTX0:CTX0 + P], PS[:, 7, 0:P],
                                ALU.mult).then_inc(xn, 1)

            def norm_rest(N):
                for t in range(KT):
                    dve.wait_ge(h_hi, N * KT + (t + 1))
                    v.tensor_tensor(H_lo[:, t, :], HF[:, t % 2, :], H_hi[:, t, :].bitcast(F32),
                                    ALU.subtract).then_inc(h_lo, 1)
                    if t + 2 < KT:
                        normalise(N, t + 2)

            def modulation(l, w):
                if w == 0:
                    t0, t1, src = 0, 16, PS[:, 2, 0:32]
                    dve.wait_ge(v_ev, l + 1)
                    dve.wait_ge(ada_sel, l * NADA + ADA_A)
                else:
                    t0, t1, src = 16, 48, PS[:, 7, 256:320]
                    dve.wait_ge(ada_sel, l * NADA + NADA)
                bias = VT[:, t0:t1].rearrange("p (t o) -> p t o", o=1).to_broadcast([P, t1 - t0, 2])
                v.tensor_tensor(MOD[:, t0:t1, :], src.rearrange("p (t o) -> p t o", o=2), bias,
                                ALU.add).then_inc(mod_ok, 1)
                dve.wait_ge(mod_ok, l * 4 + (2 * w + 1))
                gain = VT[:, 48 + KT * w:48 + KT * (w + 1)].rearrange("p (t o) -> p t o", o=1)
                s0 = 8 + 24 * w
                v.scalar_tensor_tensor(AB[:, w, :, :], MOD[:, s0:s0 + KT, :], 1.0,
                                       gain.to_broadcast([P, KT, 2]), ALU.add, ALU.mult).then_inc(mod_ok, 1)

            def residual(l, w, t, done):
                for cond, (c0, c1) in enumerate(((0, NLAT), (CTX0, CTX0 + NCTX))):
                    ins = v.scalar_tensor_tensor(X[:, t, c0:c1], DN[:, t, c0:c1],
                                                 MOD[:, 16 + 24 * w + t, cond:cond + 1], X[:, t, c0:c1],
                                                 ALU.mult, ALU.add)
                ins.then_inc(done, 1)

            with dve.Fori(0, DEPTH) as l:
                own = Chain(dve, dve_own, l * DVE_OWN)
                norm_start(l * 2)
                v.memset(KS[:, 0:TT, :, HD:P], 0.0).then_inc(zeroed, 1)
                v.memset(KS[:, PAST, :, 0:HD], 0.0).then_inc(zeroed, 1)
                v.memset(QS[:, QT, :, HD:P], 0.0).then_inc(zeroed, 1)
                modulation(l, 0)
                norm_rest(l * 2)

                dve.wait_ge(pj_ev, l * 25 + 25)
                own.then(v.tensor_tensor(HS[:, :, :], PMG[:, :, 0:384], PMG[:, :, 0:384], ALU.mult))
                own.wait()
                r30 = SS[:, 0, 0:30].rearrange("p (t h) -> p t h", h=6)
                own.then(v.tensor_reduce(r30, HS[:, :, :].rearrange("p t (h n) -> p t h n", n=HD), AXX, ALU.add))
                own.wait()
                own.then(v.tensor_tensor(HS[:, :, 0:320], PMM[:, :, 0:320], PMM[:, :, 0:320], ALU.mult))
                own.wait()
                v.tensor_reduce(SS[:, 0, 30:35], HS[:, :, 0:192], AXX, ALU.add)
                own.then(v.tensor_reduce(SS[:, 0, 35:40], HS[:, :, 192:320], AXX, ALU.add))
                own.wait()
                for c0, c1, n in ((0, 30, HD), (30, 35, QLORA), (35, 40, KVLORA)):
                    ins = v.tensor_scalar(SS[:, 0, c0:c1], SS[:, 0, c0:c1], 1.0 / n, EPS, ALU.mult, ALU.add)
                ins.then_inc(hn, 1)
                v.tensor_scalar(SK[:, :], SINK[:, :], -1.0, None, ALU.mult)
                for k in range(2):
                    ins = v.tensor_scalar(WQ[:, k, :], WQ[:, k, :], VT[0:96, 70 + k:71 + k], None, ALU.mult)
                ins.then_inc(wq_ok, 1)
                dve.wait_ge(hp, l + 1)
                for t in range(TT):
                    r = SS[:, 1, 6 * t:6 * t + 6].rearrange("p (h o) -> p h o", o=1).to_broadcast([P, 6, HD])
                    qk = PMG[:, t, 0:384].rearrange("p (h n) -> p h n", n=HD)
                    ins = v.tensor_tensor(qk, qk, r, ALU.mult)
                    v.tensor_scalar(PMM[:, t, 0:192], PMM[:, t, 0:192], SS[:, 1, 30 + t:31 + t], None, ALU.mult)
                own.then(ins)
                own.wait()
                gain = GAIN[:, 0:384].rearrange("p (o n) -> p o n", o=1).to_broadcast([P, TT, 384])
                v.tensor_tensor(PMG[:, :, 0:384], PMG[:, :, 0:384], gain, ALU.mult)
                for t in range(TT):
                    ins = v.scalar_tensor_tensor(PMM[:, t, 192:320], PMM[:, t, 192:320], SS[:, 1, 35 + t:36 + t],
                                                 GAIN[:, 384:512], ALU.mult, ALU.mult)
                ins.then_inc(head_in, 1)
                dve.wait_ge(head_in, l + 1)
                dve.wait_ge(zeroed, l * 3 + 3)
                own.then(rope(v, own.wait, own.then, lambda t: PMM[:, t, 320:352].rearrange("p (h n) -> p h n", h=1),
                              lambda t: PMM[:, t, 320:352].rearrange("p (h n) -> p h n", h=1),
                              K_C32, K_S32, 1, ROPE))
                own.wait()
                for g, pm in enumerate((PMG, PMS)):
                    ins = rope(v, own.wait, own.then, lambda t: KS[:, t, 2 * g:2 * g + 2, 0:HD],
                               lambda t: pm[:, t, 256:384].rearrange("p (h n) -> p h n", n=HD),
                               K_C64, K_S64, 2, HD)
                    if g == 0:
                        own.then(ins)
                        own.wait()
                ins.then_inc(rot_k, 1)
                dve.wait_ge(rot_k, l * 2 + 1)
                rope(v, own.wait, own.then, lambda t: QS[:, t, :, 0:HD],
                     lambda t: PMG[:, t, 0:256].rearrange("p (h n) -> p h n", n=HD),
                     K_C64, K_S64, 4, HD).then_inc(rot_q, 1)

                v.memset(TP[:, :, 0:1], 0.0)
                v.memset(TP[:, :, T + 1:T + 2], 0.0)
                dve.wait_ge(w_used, l * NW + (SPL + 14))
                dve.wait_ge(feat, l * 2 + 2)
                for o in range(2):
                    pair = (3 + o) % 4
                    ins = v.tensor_tensor(TP[:, o, 1:T + 1].rearrange("p (h n) -> p h n", h=2),
                                          PS[:, 2 * pair:2 * pair + 2, 0:HALF],
                                          GC[:, o, :].rearrange("p (h n) -> p h n", h=2), ALU.mult)
                own.then(ins)
                own.wait()
                for o in range(2):
                    own.then(v.tensor_scalar(CV[:, o, :], TP[:, o, 0:T], VT[:, 64 + o:65 + o], None, ALU.mult))
                for tap in range(1, 3):
                    for o in range(2):
                        if o == 0:
                            own.wait()
                        own.then(v.scalar_tensor_tensor(CV[:, o, :], TP[:, o, tap:tap + T],
                                                        VT[:, 64 + 2 * tap + o:65 + 2 * tap + o], CV[:, o, :],
                                                        ALU.mult, ALU.add))
                own.wait()
                dve.wait_ge(w_used, l * NW + (SPL + 16))
                for o in range(2):
                    v.tensor_tensor(CV[:, o, :].rearrange("p (h n) -> p h n", h=2), PS[:, 2 + 2 * o:4 + 2 * o, 0:HALF],
                                    CV[:, o, :].rearrange("p (h n) -> p h n", h=2), ALU.mult).then_inc(gated, 1)
                for o in range(2):
                    dve.wait_ge(ya_hi, l * 2 + (o + 1))
                    v.tensor_tensor(H_lo[:, o, :], CV[:, o, :], H_hi[:, o, :].bitcast(F32),
                                    ALU.subtract).then_inc(ya_lo, 1)

                def maximum(h, q):
                    g, j = divmod(h, 4)
                    n = SIDX[(h, q)]
                    dve.wait_ge(s_mm, l * NS_ + (n + 1))
                    mx, nb = ST[:, 0, n % 4:n % 4 + 1], ST[:, 1, n % 4:n % 4 + 1]
                    s = score_ap(h, q, n)
                    v.tensor_reduce(mx, s, mybir.AxisListType.XY if len(s.shape) == 3 else AXX,
                                    ALU.max).then_inc(s_max, 1)
                    dve.wait_ge(s_max, l * NS_ + (n + 1))
                    if g == 1:
                        v.tensor_scalar(nb, mx, -SCALES[g], SK[:, j:j + 1], ALU.mult, ALU.min).then_inc(s_nb, 1)
                    else:
                        v.tensor_scalar(nb, mx, -SCALES[g], None, ALU.mult).then_inc(s_nb, 1)

                def normalise_probs(h, q):
                    n = SIDX[(h, q)]
                    dve.wait_ge(s_exp, l * NS_ + (n + 1))
                    den, rec = ST[:, 2, n % 4:n % 4 + 1], ST[:, 3, n % 4:n % 4 + 1]
                    if h // 4 == 1:
                        dve.wait_ge(s_sink, l * 20 + (n - 20 + 1))
                        v.tensor_tensor(den, den, SE[:, n % 4:n % 4 + 1], ALU.add).then_inc(s_den, 1)
                        dve.wait_ge(s_den, l * 20 + (n - 20 + 1))
                    v.reciprocal(rec, den).then_inc(s_rec, 1)
                    dve.wait_ge(s_rec, l * NS_ + (n + 1))
                    pr = prob_ap(h, q)
                    v.tensor_scalar(pr, pr, rec, None, ALU.mult).then_inc(s_norm, 1)

                waiting = None
                for e in ORDER:
                    if e[0] == "S":
                        maximum(*e[1:])
                        if waiting:
                            normalise_probs(*waiting)
                        waiting = e[1:]
                        continue
                    if e[0] == "T" and e[1][0] == "P" and waiting and waiting[0] == e[1][1]:
                        normalise_probs(*waiting)
                        waiting = None
                    if e[0] == "T" and FILL_AT[e[1]] % 2 == 1:
                        evac_fill(dve, copy, l, e[1])
                    elif e == ("PREP", 2):
                        dve.wait_ge(tr_mm, l * NFILL + (FILL_AT[("K", 3, 1)] + 1))
                        for t in range(QT):
                            copy(KS[:, t, :, HD:96],
                                 PMM[:, t, 320:352].rearrange("p (o n) -> p o n", o=1).to_broadcast([P, 4, ROPE]))
                        v.memset(KS[:, PAST, :, HD:96], 0.0).then_inc(rot_k, 1)
                    elif e[0] == "V" and e[2] in (TT, QT):
                        h, k = e[1:]
                        yi, r0, (c0, c1) = 2 * h + (k != TT), HD * (h % 2), y_cols(k)
                        tile = YTILE[h // 4] + h % 4 // 2
                        dve.wait_ge(y_hi, l * (2 * HEADS) + (yi + 1))
                        v.tensor_tensor(H_lo[r0:r0 + HD, tile, c0:c1], PS[r0:r0 + HD, 6, 0:c1 - c0],
                                        H_hi[r0:r0 + HD, tile, c0:c1].bitcast(F32), ALU.subtract).then_inc(y_lo, 1)
                    if waiting:
                        normalise_probs(*waiting)
                        waiting = None
                modulation(l, 1)

                for t in range(KT):
                    dve.wait_ge(o_ev, l * NOUT + (t + 2))
                    residual(l, 0, t, x_mid)
                norm_start(l * 2 + 1)
                norm_rest(l * 2 + 1)
                for t in range(KT):
                    ins = v.memset(DN[:, t, :], 0.0)
                own.then(ins)
                v.memset(U[:, :, :, 0:1], 0.0)
                own.then(v.memset(U[:, :, :, T + 1:T + 2], 0.0))
                own.wait()

                def convolve(i, ch, s, column, first):
                    dve.wait_ge(up_ev, l * 44 + i * 4 + (2 * ch + s + 1))
                    if not first:
                        dve.wait_ge(g_hi, l * 22 + i * 2 + (ch + 1 - 2))
                        dve.wait_ge(g_lo, l * 22 + i * 2 + (ch + 1 - 2))
                    x = 2 * (2 * ch + s)
                    v.tensor_scalar(CF[:, ch, s, :], U[:, ch, s, 0:T], column(0), None, ALU.mult).then_inc(cv_own, 1)
                    dve.wait_ge(cv_own, l * 88 + i * 8 + (x + 1))
                    v.scalar_tensor_tensor(CF[:, ch, s, :], U[:, ch, s, 1:T + 1], column(1), CF[:, ch, s, :],
                                           ALU.mult, ALU.add).then_inc(cv_own, 1)
                    dve.wait_ge(cv_own, l * 88 + i * 8 + (x + 2))
                    v.scalar_tensor_tensor(CF[:, ch, s, :], U[:, ch, s, 2:T + 2], column(2), CF[:, ch, s, :],
                                           ALU.mult, ALU.add).then_inc(cv_done, 1)

                def gate(i, ch):
                    dve.wait_ge(silu_ok, l * 22 + i * 2 + (ch + 1))
                    dve.wait_ge(cv_done, l * 44 + i * 4 + (2 * ch + 2))
                    v.tensor_tensor(CF[:, ch, 1, :], CF[:, ch, 1, :], CF[:, ch, 0, :], ALU.mult).then_inc(g_f, 1)

                def g_low(i, ch, slot):
                    dve.wait_ge(g_hi, l * 22 + i * 2 + (ch + 1))
                    v.tensor_tensor(G_lo[:, slot, ch, :], CF[:, ch, 1, :], G_hi[:, slot, ch, :].bitcast(F32),
                                    ALU.subtract).then_inc(g_lo, 1)

                def down_add(q, used, before):
                    dve.wait_ge(w_used, used)
                    dve.wait_ge(dn_add, before)
                    for t in range(4):
                        out = DN[:, 4 * q + t, :].rearrange("p (h n) -> p h n", h=2)
                        v.tensor_tensor(out, PS[:, 2 * t:2 * t + 2, 0:HALF], out, ALU.add).then_inc(dn_add, 1)

                for ch in range(2):
                    for s in range(2):
                        convolve(0, ch, s, lambda tap: VT[:, 72 + 44 * tap + 22 * s + ch:73 + 44 * tap + 22 * s + ch], True)
                for ch in range(2):
                    gate(0, ch)
                    g_low(0, ch, 0)
                s0 = NPROJ + NOUT + 4
                with dve.Fori(0, PAIRS // 2) as m:
                    for b_ in range(2):
                        i = m * 2 + (1 + b_)
                        for ch in range(2):
                            for s in range(2):
                                convolve(i, ch, s, lambda tap: VT[:, bass.ds(
                                    m * 4 + (72 + 44 * tap + 22 * s + 2 * (1 + b_) + ch), 1)], False)

                        def add_i(q):
                            down_add(q, l * NW + m * 12 + (SPL + s0 + 6 * b_ + 5 + q),
                                     l * (8 * PAIRS) + i * 8 + 4 * q)
                        gate(i, 0)
                        g_low(i, 0, (1 + b_) % 2)
                        add_i(0)
                        gate(i, 1)
                        add_i(1)
                        g_low(i, 1, (1 + b_) % 2)
                for q in range(2):
                    down_add(q, l * NW + (SPL + NW - 1 + q), l * (8 * PAIRS) + (8 * PAIRS + 4 * q))
                dve.wait_ge(dn_add, l * (8 * PAIRS) + (8 * PAIRS + 8))
                for t in range(KT):
                    residual(l, 1, t, x_fin)
                assert own.n == DVE_OWN, own.n

            norm_start(2 * DEPTH)
            for t in range(2, KT):
                normalise(2 * DEPTH, t)


_INS = ['x_prompt', 'x_sample', 'cache_mla_ckv', 'cache_mla_kpe', 'cache_gqa_k', 'cache_gqa_v', 'cache_swa_k',
        'cache_swa_v', 'c', 'c_ctx', 'w_ada', 'b_ada', 'norm1', 'w_in', 'conv_a', 'mla_q_norm', 'mla_wq_b',
        'mla_kv_norm', 'mla_wkv_b', 'gqa_q_norm', 'gqa_k_norm', 'swa_sink', 'w_out', 'norm2', 'w_up', 'conv_ff',
        'w_down', 'final_norm']
_OUTS = [((1, NCTX, D), 'float32'), ((1, NLAT, D), 'float32'), ((1, DEPTH, NCTX, KVLORA), 'float32'),
         ((1, DEPTH, NCTX, ROPE), 'float32')] + [((1, DEPTH, NCTX, 2, HD), 'float32')] * 4


def constants():
    k = np.zeros((P, K_N), np.float32)
    i, n = np.arange(P)[:, None], np.arange(P)[None, :]
    k[:, K_ID:K_ID + P] = i == n
    k[:, K_MASK:K_MASK + P] = np.where(n < i, NEG, 0)
    k[:, K_MASK + P:K_MASK + 2 * P] = np.where(n > i, NEG, 0)
    k[:, K_ONE:K_ONE + P] = 1
    for cond in range(2):
        k[np.arange(4) * 32 + cond, K_SEL + cond] = 1
    pos = np.arange(NLAT)
    for dim, kc, ks in ((HD, K_C64, K_S64), (ROPE, K_C32, K_S32)):
        half = dim // 2
        inv = np.power(np.float32(10000.0), -np.arange(0, half, 2, dtype=np.float32) / np.float32(half))
        row = (pos // GRID_W).astype(np.float32)[:, None] * inv
        col = (pos % GRID_W).astype(np.float32)[:, None] * inv
        cos = np.concatenate([np.cos(row)] * 2 + [np.cos(col)] * 2, axis=1)
        sin = np.concatenate([-np.sin(row), np.sin(row), -np.sin(col), np.sin(col)], axis=1)
        for t in range(QT):
            k[:, kc + dim * t:kc + dim * (t + 1)] = cos[P * t:P * (t + 1)]
            k[:, ks + dim * t:ks + dim * (t + 1)] = sin[P * t:P * (t + 1)]
    k[:, K_MH:K_MH + 40] = -0.5
    return k


def kernel(**inputs):
    import numpy as _np
    import concourse.bacc as _bacc
    from concourse import mybir as _mybir
    from concourse.bass_utils import run_bass_kernel_spmd as _run

    nc = _bacc.Bacc("TRN2", target_bir_lowering=False, num_devices=1)
    arrays, args = {}, []
    for name in _INS + ["consts"]:
        a = constants() if name == "consts" else _np.ascontiguousarray(inputs[name])
        arrays[f"in_{name}_dram"] = a
        args.append(nc.dram_tensor(f"in_{name}_dram", a.shape, _mybir.dt.from_np(a.dtype), kind="ExternalInput").ap())
    for i, (shape, dtype) in enumerate(_OUTS):
        dt = _mybir.dt.from_np(_np.dtype(dtype))
        args.append(nc.dram_tensor(f"out_{i}_dram", shape, dt, kind="ExternalOutput").ap())
    backbone_program(nc, *args)
    r = _run(nc, [arrays], core_ids=[0])
    return tuple(r.results[0][f"out_{i}_dram"] for i in range(len(_OUTS)))
```

```python
from contextlib import ExitStack

import numpy as np

import concourse.bass as bass
from concourse import mybir

F32 = mybir.dt.float32
F32R = mybir.dt.float32r
ACT = mybir.ActivationFunctionType
ALU = mybir.AluOpType
AXX = mybir.AxisListType.X

P = 128
D = 1024
DEPTH = 2
KT = D // P
NLAT, NCTX = 512, 128
QT = NLAT // P
CTX0 = NLAT + 2
T = CTX0 + NCTX + 2
HALF = T // 2
TILE0 = [P * i for i in range(QT)] + [CTX0]
TT = QT + 1
HD = 64
GRID_W = 64
FF = 2816
FT = FF // P
PAIRS = FT // 2
EPS = 1e-6
NEG = -1e30
SCALES = [HD ** -0.5, HD ** -0.5, 96 ** -0.5]
YTILE = [4, 6, 2]
QLORA, KVLORA, ROPE = 192, 128, 32
KEYS = P + NLAT + P
C_LAT, C_CTX = P, P + NLAT
NADA = 24
ADA_A = 8

TOKEN_CHUNKS = [(1120, 256), (1376, 256), (768, 352), (1632, 256), (1888, 256)]
FEAT_CHUNKS = [512, 0, 256]
NPROJ = 2 * (len(TOKEN_CHUNKS) + len(FEAT_CHUNKS))
NOUT = 8
NFF = 6 * PAIRS
NW = NPROJ + NOUT + NFF
NRAW = 2 * NADA + NW
RAW, SPL = 3, 2
RMAX = 4 * 352

K_ID, K_MASK, K_ONE, K_SEL = 0, 128, 384, 512
K_C64, K_S64, K_C32, K_S32 = 514, 770, 1026, 1154
K_MH, K_N = 1282, 1322
HALFK = (P + NLAT) // 2


def raw_of_split(s):
    if s == 0:
        return 2 * ADA_A - 2
    return 2 * ADA_A + s if s < NPROJ else 2 * NADA + s


def raw_of_ada(a):
    if a < 2 * ADA_A:
        return a if a < 2 * ADA_A - 2 else a + 1
    return NPROJ + a


RAW_KIND = {}
for _s in range(NW):
    RAW_KIND[raw_of_split(_s)] = ("w", _s)
for _a in range(2 * NADA):
    RAW_KIND[raw_of_ada(_a)] = ("ada", _a)
assert sorted(RAW_KIND) == list(range(NRAW)) and NRAW % RAW == 0 and NW % SPL == 0


HEADS = 12
NQ = TT
PAST = TT
NVEC, NATT = 7, 16


def kv_of(h):
    return h - 4 if h >= 8 else 2 * (h // 4) + (h % 4) // 2


def window(h, q):
    return (max(q - 1, 0), min(q + 2, QT)) if h // 4 == 1 else (0, QT)


def queries(h, k):
    if k == 0 or h // 4 != 1:
        return 0, QT
    return max(k - 2, 0), min(k + 1, QT)


def prob_col(h, q, k):
    return 0 if k == 0 or q == QT else P * (k - window(h, q)[0])


P_SEQ = [TT] + list(range(TT))


def attention_order():
    order = []

    def probs(h):
        return [("T", ("P", h, k)) for k in P_SEQ], [("V", h, k) for k in P_SEQ]
    mla = []
    for i in range(TT + 2):
        mla += [("T", ("MT", i))] if i < TT + 1 else []
        mla += [("T", ("MQ", i - 1))] if 1 <= i <= TT else []
        mla += [("T", ("MV", i - 1))] if i >= 1 else []
    ch = ADA_A
    late = []
    for h in range(HEADS):
        t, v = probs(h - 1) if h else ([], [])
        if h == 8:
            order += t[:1] + late + t[1:2]
            for x in range(2, len(t)):
                order += v[x - 2:x - 1] + t[x:x + 1]
            order += v[-2:]
            t, v, late = [], [], []
        if h == 0 or kv_of(h) != kv_of(h - 1):
            order += [("T", ("K", kv_of(h), 0)), ("T", ("K", kv_of(h), 1))]
        order += late + [("T", ("Q", h, 0)), ("T", ("Q", h, 1))]
        if h == 3:
            order.append(("PREP", 1))
        todo = [ch] + ([ch + 1] if h % 3 == 0 else [])
        ch += len(todo)
        order += [("ADA", todo[0])] + t[:1]
        for q in range(NQ):
            order.append(("S", h, q))
            order += t[q + 1:q + 2] + v[q:q + 1]
            if q == 0:
                order.append(("MOVE", todo[0]))
            if q == 1:
                order.append(("SEL", todo[0]))
            if h == 7:
                order += mla[3 * q:3 * q + 3]
            if q == 3 and len(todo) > 1:
                order.append(("ADA", todo[1]))
        late = v[5:]
        if len(todo) > 1:
            order += [("MOVE", todo[1]), ("SEL", todo[1])]
        if h == 7:
            order += mla[15:] + [("PREP", 2)]
    t, v = probs(HEADS - 1)
    order += late + t[:2]
    for x in range(2, len(t)):
        order += v[x - 2:x - 1] + t[x:x + 1]
    order += v[-2:]
    assert ch == NADA
    return order


ORDER = attention_order()
FILLS = [e[1] for e in ORDER if e[0] == "T"]
FILL_AT = {key: n for n, key in enumerate(FILLS)}
assert len(FILLS) == len(FILL_AT)
NFILL = len(FILLS)
NEV = [(NFILL + 1) // 2, NFILL // 2]
NS_ = NQ * HEADS
SIDX = {e[1:]: n for n, e in enumerate(x for x in ORDER if x[0] == "S")}
assert all(SIDX[(h, q)] == NQ * h + q for h in range(HEADS) for q in range(NQ))


def by_scalar(key):
    return key[0] == "P"


class Chain:

    def __init__(self, eng, sem, base):
        self.eng, self.sem, self.base, self.n = eng, sem, base, 0

    def then(self, ins):
        ins.then_inc(self.sem, 1)
        self.n += 1

    def wait(self):
        self.eng.wait_ge(self.sem, self.base + self.n)


DVE_OWN = 28


def backbone_program(nc, x_prompt, x_sample, cache_mla_ckv, cache_mla_kpe, cache_gqa_k, cache_gqa_v,
                     cache_swa_k, cache_swa_v, c, c_ctx, w_ada, b_ada, norm1, w_in, conv_a, mla_q_norm,
                     mla_wq_b, mla_kv_norm, mla_wkv_b, gqa_q_norm, gqa_k_norm, swa_sink, w_out, norm2,
                     w_up, conv_ff, w_down, final_norm, consts,
                     y_prompt, y_sample, new_ckv, new_kpe, new_gk, new_gv, new_sk, new_sv):
    ctx = ExitStack()
    with ctx:
        def sb(name, shape, dt=F32, stack=ctx):
            return stack.enter_context(nc.sbuf_tensor(name, shape, dt))

        def sem(name):
            return ctx.enter_context(nc.semaphore(name))

        X = sb("X", [P, KT, T])
        H_hi = sb("H_hi", [P, KT, T], F32R)
        H_lo = sb("H_lo", [P, KT, T], F32R)
        RW = sb("RW", [P, RAW, RMAX])
        W_hi = sb("W_hi", [P, SPL, RMAX], F32R)
        W_lo = sb("W_lo", [P, SPL, RMAX], F32R)
        K = sb("K", [P, K_N])
        VT = sb("VT", [P, 72 + 132])
        MOD = sb("MOD", [P, 48, 2])
        AB = sb("AB", [P, 2, KT, 2])
        CT = sb("CT", [P, KT, 32])
        R = sb("R", [P, 256])
        NS = sb("NS", [P, 2, 8])
        FN = sb("FN", [P, KT])
        SS = sb("SS", [P, 2, 40])
        ST = sb("ST", [P, 4, 4])
        SK = sb("SK", [P, 4])
        SE = sb("SE", [P, 4])
        IDENT = K[:, K_ID:K_ID + P]
        ONES = K[:, K_ONE:K_ONE + P]
        SINK = sb("SINK", [P, 4])
        GAIN = sb("GAIN", [P, 6 * HD + KVLORA])
        CX = sb("CX", [P, 160 + 4 * P])
        WQ = sb("WQ", [96, 2, 384])
        WK = sb("WK", [P, 512])

        b = ExitStack()
        PR = sb("PR", [P, 2, QT * (P + NLAT) + P], F32, b)
        PT = sb("PT", [P, 2, NLAT], F32, b)
        QTR = sb("QTR", [P, 2, NQ * P], F32, b)
        b.close()
        b = ExitStack()
        SQ = sb("SQ", [P, 2, T], F32, b)
        SUM = sb("SUM", [P, T], F32, b)
        XN = sb("XN", [P, 2, T], F32, b)
        HF = sb("HF", [P, 2, T], F32, b)
        DG = sb("DG", [P, TT, P], F32, b)
        U = sb("U", [P, 2, 2, T + 2], F32, b)
        b.close()
        b = ExitStack()
        GC = sb("GC", [P, 2, T], F32, b)
        TP = sb("TP", [P, 2, T + 2], F32, b)
        CV = sb("CV", [P, 2, T], F32, b)
        HS = sb("HS", [P, TT, 384], F32, b)
        VR = sb("VR", [70, P], F32, b)
        VF = sb("VF", [66, 2, P], F32, b)
        VQ = sb("VQ", [2, 96], F32, b)
        sb("rest", [P, 1560 - 96], F32, b)

        a = ExitStack()
        PMG = sb("PMG", [P, TT, 512], F32, a)
        PMS = sb("PMS", [P, TT, 512], F32, a)
        PMM = sb("PMM", [P, TT, 352], F32, a)
        QS = sb("QS", [P, TT, 4, P], F32, a)
        KS = sb("KS", [P, TT + 1, 4, P], F32, a)
        KTR = sb("KTR", [P, 2, KEYS], F32, a)
        t = ExitStack()
        TA = sb("TA", [P, 2, 4 * HD], F32, t)
        TB = sb("TB", [P, 2, 4 * HD], F32, t)
        t.close()
        t = ExitStack()
        CQ = sb("CQ", [P, 2, 3, P], F32, t)
        t.close()
        a.close()
        a = ExitStack()
        CF = sb("CF", [P, 2, 2, T], F32, a)
        G_hi = sb("G_hi", [P, 2, 2, T], F32R, a)
        G_lo = sb("G_lo", [P, 2, 2, T], F32R, a)
        DN = sb("DN", [P, KT, T], F32, a)
        a.close()
        a = ExitStack()
        XIN = sb("XIN", [P, TT, D], F32, a)
        CR = sb("CR", [16, P], F32, a)
        FR = sb("FR", [KT, P], F32, a)
        a.close()
        a = ExitStack()
        YO = sb("YO", [P, KT, T], F32, a)
        OUT = sb("OUT", [P, TT, D], F32, a)
        a.close()
        b.close()

        PS = ctx.enter_context(nc.psum_tensor("PS", [P, 8, 512], F32))

        const_in, c_in, f_in = sem("const_in"), sem("c_in"), sem("f_in")
        x_in = [sem(f"x_in{i}") for i in range(TT)]
        vec_in, att_in, u_free = sem("vec_in"), sem("att_in"), sem("u_free")
        raw_in = [sem(f"raw_in{i}") for i in range(RAW)]
        setup_v, x_tr, x_ev = sem("setup_v"), sem("x_tr"), sem("x_ev")
        c_tr, c_silu, f_tr, f_ev = sem("c_tr"), sem("c_silu"), sem("f_tr"), sem("f_ev")
        v_tr, v_ev = sem("v_tr"), sem("v_ev")
        ada_mm, ada_ev, ada_sel, mod_ok = sem("ada_mm"), sem("ada_ev"), sem("ada_sel"), sem("mod_ok")
        w_hi, w_lo, w_used = sem("w_hi"), sem("w_lo"), sem("w_used")
        sq_done, ss_add, st_mm, nv, rv, dg, bc_mm = (sem(n) for n in (
            "sq_done", "ss_add", "st_mm", "nv", "rv", "dg", "bc_mm"))
        xn, hf, h_hi, h_lo = sem("xn"), sem("hf"), sem("h_hi"), sem("h_lo")
        pj_ev, feat, gated, ya_hi, ya_lo = (sem(n) for n in ("pj_ev", "feat", "gated", "ya_hi", "ya_lo"))
        hn, hp, head_in, zeroed = sem("hn"), sem("hp"), sem("head_in"), sem("zeroed")
        raw_q, raw_k, rot_q, rot_k, rot_own, wq_ok = (sem(n) for n in (
            "raw_q", "raw_k", "rot_q", "rot_k", "rot_own", "wq_ok"))
        tr_mm = sem("tr_mm")
        tr_ev = [sem("tr_ev_4"), sem("tr_ev_5")]
        s_mm, s_max, s_nb, s_exp, s_sink, s_den, s_rec, s_norm = (sem(n) for n in (
            "s_mm", "s_max", "s_nb", "s_exp", "s_sink", "s_den", "s_rec", "s_norm"))
        pv_mm, y_hi, y_lo = sem("pv_mm"), sem("y_hi"), sem("y_lo")
        new_out, x_mid, x_fin = sem("new_out"), sem("x_mid"), sem("x_fin")
        up_ev, cv_own, cv_done, silu_ok, g_f, g_hi, g_lo = (sem(n) for n in (
            "up_ev", "cv_own", "cv_done", "silu_ok", "g_f", "g_hi", "g_lo"))
        dn_mm, dn_add, dve_own = sem("dn_mm"), sem("dn_add"), sem("dve_own")
        fin_y, fin_tr, y_out = sem("fin_y"), sem("fin_tr"), sem("y_out")
        fin_ev = [sem("fin_ev_dve"), sem("fin_ev_act")]

        block = ctx.enter_context(nc.Block())

        def v_ap(g, kv, tile):
            if g == 2:
                return PMG[:, kv, 384:384 + HD] if tile == PAST else PMS[:, tile, HD * kv:HD * (kv + 1)]
            if tile == PAST:
                return CX[:, 288 + 256 * g + HD * kv:288 + 256 * g + HD * (kv + 1)]
            return (PMG, PMS)[g][:, tile, 384 + HD * kv:384 + HD * (kv + 1)]

        def score_ap(h, q, n):
            if q == QT:
                return PS[:, 2 * (n % 2), 0:P]
            if h // 4 == 1:
                lo, hi = window(h, q)
                return PS[:, 2 * (n % 2), 0:P * (1 + hi - lo)]
            return PS[:, 2 * (n % 2):2 * (n % 2) + 2, 0:HALFK]

        def prob_ap(h, q):
            c0 = q * (P + NLAT)
            if q == QT:
                return PR[:, h % 2, c0:c0 + P]
            if h // 4 == 1:
                lo, hi = window(h, q)
                return PR[:, h % 2, c0:c0 + P * (1 + hi - lo)]
            return PR[:, h % 2, c0:c0 + P + NLAT].rearrange("p (b n) -> p b n", n=HALFK)

        def y_cols(k):
            return (CTX0, CTX0 + P) if k == TT else (0, NLAT)

        def evac_fill(eng, copy, l, key):
            n = FILL_AT[key]
            bank = PS[:, 4 + n % 2, :]
            eng.wait_ge(tr_mm, l * NFILL + (n + 1))
            done = tr_ev[n % 2]
            kind = key[0]
            if kind == "P":
                _, h, k = key
                i = 6 * h + P_SEQ.index(k)
                if i >= 2:
                    eng.wait_ge(pv_mm, l * 6 * HEADS + i - 1)
                c0, c1 = (0, P) if k == TT else (P * queries(h, k)[0], P * queries(h, k)[1])
                copy(PT[:, i % 2, c0:c1], bank[:, c0:c1]).then_inc(done, 1)
            elif kind == "Q":
                _, h, part = key
                if h >= 2:
                    eng.wait_ge(s_mm, l * NS_ + NQ * (h - 1))
                c0, c1 = (0, NLAT) if part == 0 else (NLAT, NLAT + P)
                copy(QTR[:, h % 2, c0:c1], bank[:, 0:c1 - c0]).then_inc(done, 1)
            elif kind == "K":
                _, kv, part = key
                if kv >= 2:
                    last = max(h for h in range(HEADS) if kv_of(h) == kv - 2)
                    eng.wait_ge(s_mm, l * NS_ + NQ * (last + 1))
                c0, c1 = (0, 512) if part == 0 else (512, KEYS)
                copy(KTR[:, kv % 2, c0:c1], bank[:, 0:c1 - c0]).then_inc(done, 1)
            elif kind == "MT":
                i = key[1]
                if i >= 2:
                    eng.wait_ge(tr_mm, l * NFILL + (FILL_AT[("MV", i - 2)] + 1))
                else:
                    eng.wait_ge(rot_q, l * 3 + 2)
                if i < TT:
                    copy(CQ[0:96, i % 2, 0:2, :], bank[0:96, 0:2 * P].rearrange("p (k n) -> p k n", n=P))
                copy(CQ[:, i % 2, 2, :], bank[:, 2 * P:3 * P]).then_inc(done, 1)
            elif kind == "MQ":
                eng.wait_ge(new_out, l * 96 + 96)
                copy(PMG[:, key[1], 0:384], bank[:, 0:384]).then_inc(done, 1)
            else:
                src = bank.rearrange("p (h n) -> p h n", n=P)
                copy(KS[:, key[1], :, 0:HD], src[:, :, 0:HD])
                eng.wait_ge(new_out, l * 96 + 96)
                eng.wait_ge(raw_q, l * 3 + 2)
                i = key[1]
                dst = PMG[:, 0:4, 384:384 + HD] if i == PAST else \
                    PMS[:, i, 0:4 * HD].rearrange("p (h n) -> p h n", n=HD)
                copy(dst, src[:, :, HD:P]).then_inc(done, 1)

        def rope(eng, wait, done, dst, src, table_c, table_s, heads, dim):
            q4, w = dim // 4, heads * dim

            def by_head(ap):
                return ap.rearrange("p (h n) -> p h n", h=heads)

            def spread(c0, n):
                return K[:, c0:c0 + n].rearrange("p (o n) -> p o n", o=1).to_broadcast([P, heads, n])
            for t0 in range(0, QT, 2):
                for t in (t0, t0 + 1):
                    eng.tensor_tensor(by_head(TA[:, t - t0, 0:w]), src(t), spread(table_c + dim * t, dim), ALU.mult)
                    for r in range(4):
                        o, i = q4 * r, q4 * (r ^ 1)
                        ins = eng.tensor_tensor(by_head(TB[:, t - t0, 0:w])[:, :, o:o + q4], src(t)[:, :, i:i + q4],
                                                spread(table_s + dim * t + o, q4), ALU.mult)
                done(ins)
                wait()
                for t in (t0, t0 + 1):
                    ins = eng.tensor_tensor(dst(t), by_head(TA[:, t - t0, 0:w]), by_head(TB[:, t - t0, 0:w]), ALU.add)
                if t0 + 2 < QT:
                    done(ins)
                    wait()
            return ins

        def all_moved(sync, l, kind):
            for b in range(2):
                own = [n for n in range(b, NFILL, 2) if FILLS[n][0] == kind]
                if own:
                    sync.wait_ge(tr_ev[b], l * NEV[b] + (max(own) // 2 + 1))

        def rope_queries(eng, sync, l, g):
            sync.wait_ge(tr_mm, l * NFILL + (FILL_AT[("Q", 4 * g - 1, 1)] + 1))
            if g == 1:
                sync.wait_ge(rot_q, l * 3 + 1)
                src, dst, dim = (lambda t: PMS[:, t, 0:256].rearrange("p (h n) -> p h n", n=HD)), \
                    (lambda t: QS[:, t, :, 0:HD]), HD
            else:
                sync.wait_ge(tr_mm, l * NFILL + (FILL_AT[("MV", TT)] + 1))
                all_moved(sync, l, "MQ")
                src, dst, dim = (lambda t: PMG[:, t, 0:384].rearrange("p (h n) -> p h n", n=96)[:, :, HD:96]), \
                    (lambda t: QS[:, t, :, HD:96]), ROPE
            tc, ts = (K_C64, K_S64) if dim == HD else (K_C32, K_S32)
            own = Chain(sync, rot_own, l * 6 + 3 * (g - 1))
            rope(eng, own.wait, own.then, dst, src, tc, ts, 4, dim).then_inc(rot_q, 1)

        @block.sync
        def _(sp):
            sp.dma_start(K[:, :], consts).then_inc(const_in, 16)
            for i in range(TT):
                src = x_sample[0, P * i:P * (i + 1), :] if i < QT else x_prompt[0, :, :]
                sp.dma_start(XIN[:, i, :], src).then_inc(x_in[i], 16)
            sp.dma_start(CR[0:8, :], c.rearrange("a (k p) -> (a k) p", p=P)).then_inc(c_in, 16)
            sp.dma_start(CR[8:16, :], c_ctx.rearrange("(k p) -> k p", p=P)).then_inc(c_in, 16)
            sp.dma_start(FR[:, :], final_norm.rearrange("(k p) -> k p", p=P)).then_inc(f_in, 16)

            def load_raw(l, r, src):
                dst = RW[:, r % RAW, 0:src.shape[1] * src.shape[2]]
                sp.dma_start(dst.rearrange("p (k n) -> p k n", n=src.shape[2]), src).then_inc(raw_in[r % RAW], 16)

            def slot_free(l, r):
                kind, n = RAW_KIND[r - RAW] if r >= RAW else ("w", r - RAW)
                if kind == "ada":
                    value = l * (2 * NADA) + (n + 1)
                else:
                    value = l * NW + (RAW + n + 1)
                sp.wait_ge(ada_mm if kind == "ada" else w_lo, value)

            def up_src(l, j, s):
                v = w_up[bass.ds(l, 1), :, bass.ds(j * P + s * FF, P)]
                return v.rearrange("a (k p) n -> p (a k) n", p=P)

            def down_src(l, i, q):
                v = w_down[bass.ds(l, 1), bass.ds(i * (2 * P), 2 * P), 512 * q:512 * (q + 1)]
                return v.rearrange("a (k p) n -> p (a k) n", p=P)

            with sp.Fori(0, DEPTH) as l:
                def small(dst, src, landed):
                    sp.dma_start(dst, src).then_inc(landed, 16)

                def row(v, p=P):
                    return v[bass.ds(l, 1), :].rearrange("a (k p) -> (a k) p", p=p)

                def vectors():
                    sp.wait_ge(u_free, l + 1)
                    small(VR[0:48, :], row(b_ada), vec_in)
                    small(VR[48:56, :], row(norm1), vec_in)
                    small(VR[56:64, :], row(norm2), vec_in)
                    small(VR[64:70, :], conv_a[bass.ds(l, 1), :, :].rearrange("a t (k p) -> (a t k) p", p=P), vec_in)
                    small(VQ[:, :], row(mla_q_norm, 96), vec_in)
                    cf = conv_ff.rearrange("l t (k p) -> l (t k) p", p=P)
                    for s in range(2):
                        small(VF[:, s, :], cf[bass.ds(l, 1), 66 * s:66 * (s + 1), :].rearrange("a r p -> (a r) p"),
                              vec_in)

                def attention_small():
                    out = [(SINK[:, :], swa_sink[bass.ds(l, 1), :].to_broadcast([P, 4]))]
                    for j in range(6):
                        g = gqa_q_norm if j < 4 else gqa_k_norm
                        out.append((GAIN[:, HD * j:HD * (j + 1)], g[bass.ds(l, 1), :].to_broadcast([P, HD])))
                    out.append((GAIN[:, 6 * HD:], mla_kv_norm[bass.ds(l, 1), :].to_broadcast([P, KVLORA])))
                    out.append((WQ[:, :, :], mla_wq_b[bass.ds(l, 1), :, :].rearrange("a (k p) n -> p (a k) n", p=96)))
                    out.append((CX[:, 0:128], cache_mla_ckv[0, bass.ds(l, 1), :, :].rearrange("a t n -> (a t) n")))
                    out.append((CX[:, 128:160], cache_mla_kpe[0, bass.ds(l, 1), :, :].rearrange("a t n -> (a t) n")))
                    for j, v in enumerate((cache_gqa_k, cache_gqa_v, cache_swa_k, cache_swa_v)):
                        out.append((CX[:, 160 + P * j:160 + P * (j + 1)],
                                    v[0, bass.ds(l, 1), :, :, :].rearrange("a t h n -> (a t) (h n)")))
                    out.append((WK[:, :], mla_wkv_b[bass.ds(l, 1), :, :].rearrange("a p n -> (a p) n")))
                    assert len(out) == NATT
                    return out
                att = attention_small()
                for r in range(2 * NADA + NPROJ + NOUT):
                    kind, n = RAW_KIND[r]
                    ch, kh = divmod(n, 2)
                    if kind == "ada":
                        src = w_ada[bass.ds(l, 1), 512 * kh:512 * (kh + 1), 256 * ch:256 * (ch + 1)]
                    elif n < NPROJ:
                        c0, w = (TOKEN_CHUNKS + [(c_, 256) for c_ in FEAT_CHUNKS])[ch]
                        src = w_in[bass.ds(l, 1), 512 * kh:512 * (kh + 1), c0:c0 + w]
                    else:
                        ch, kh = ch - NPROJ // 2, 1 - kh
                        src = w_out[bass.ds(l, 1), 512 * kh:512 * (kh + 1), 256 * ch:256 * (ch + 1)]
                    src = src.rearrange("a (k p) n -> p (a k) n", p=P)
                    if kind == "w" and n in (12, NPROJ + 1):
                        flat = (w_in if n == 12 else w_out).rearrange("l r n -> (l r) n")
                        src = flat[bass.ds(l * D, D // 2), 0:2 * P].rearrange("(k p) n -> p k n", p=P)
                    slot_free(l, r)
                    load_raw(l, r, src)
                    if r == RAW - 1:
                        vectors()
                    if r == 2 * ADA_A:
                        sp.wait_ge(x_mid, l * KT + 1)
                    if 2 * ADA_A <= r < 2 * ADA_A + NATT // 4:
                        for x in range(4):
                            small(*att[4 * (r - 2 * ADA_A) + x], att_in)
                    if r == 2 * ADA_A + NPROJ + 3:
                        sp.wait_ge(head_in, l + 1)
                        for dst, src in (
                                (new_ckv, PMM[:, QT, QLORA:QLORA + KVLORA]),
                                (new_kpe, PMM[:, QT, QLORA + KVLORA:]),
                                (new_gk, PMG[:, QT, 256:384]), (new_gv, PMG[:, QT, 384:512]),
                                (new_sk, PMS[:, QT, 256:384]), (new_sv, PMS[:, QT, 384:512])):
                            d = dst[0, bass.ds(l, 1)]
                            d = d.rearrange("a t n -> (a t) n") if len(d.shape) == 3 else \
                                d.rearrange("a t h n -> (a t) (h n)")
                            sp.dma_start(d, src).then_inc(new_out, 16)
                base = 2 * NADA + NPROJ + NOUT
                for e in range(4):
                    src = up_src(l, e // 2, e % 2)
                    slot_free(l, base + e)
                    load_raw(l, base + e, src)
                with sp.Fori(1, PAIRS) as i:
                    for e in range(6):
                        src = up_src(l, i * 2 + e // 2, e % 2) if e < 4 else down_src(l, i - 1, e - 4)
                        sp.wait_ge(w_lo, l * NW + i * 6 + (3 + NPROJ + NOUT + 4 - 6 + e - RAW + 1))
                        load_raw(l, base + 4 + e, src)
                for q in range(2):
                    src = down_src(l, PAIRS - 1, q)
                    slot_free(l, NRAW - 2 + q)
                    load_raw(l, NRAW - 2 + q, src)
            sp.wait_ge(new_out, 96 * DEPTH)
            for i in range(TT):
                sp.wait_ge(fin_ev[0], i + 1)
                sp.wait_ge(fin_ev[1], i + 1)
                dst = y_sample[0, P * i:P * (i + 1), :] if i < QT else y_prompt[0, :, :]
                sp.dma_start(dst, OUT[:, i, :]).then_inc(y_out, 16)
            sp.wait_ge(y_out, 16 * TT)

        @block.gpsimd
        def _(pool):
            pool.sem_inc(w_lo, RAW)
            pool.sem_inc(w_used, SPL)
            pool.sem_inc(x_mid, 1)
            pool.sem_inc(u_free, 1)
            pool.sem_inc(dn_add, 8)
            pool.wait_ge(const_in, 16)

            def low(value, slot, raw, width):
                pool.wait_ge(w_hi, value)
                nc.gpsimd.tensor_tensor(W_lo[:, slot, 0:width], RW[:, raw, 0:width],
                                        W_hi[:, slot, 0:width].bitcast(F32), ALU.subtract).then_inc(w_lo, 1)

            def item(l, s):
                low(l * NW + (s + 1), s % SPL, raw_of_split(s) % RAW, RMAX if s in (4, 5) else 1024)

            def norm_root(N):
                pool.wait_ge(nv, N + 1)
                nc.gpsimd.tensor_tensor(NS[:, 1, 0:TT], NS[:, 0, 0:TT], K[:, K_MH:K_MH + TT],
                                        ALU.pow).then_inc(rv, 1)

            with pool.Fori(0, DEPTH) as l:
                norm_root(l * 2)
                for s in range(9):
                    item(l, s)
                pool.wait_ge(hn, l + 1)
                nc.gpsimd.tensor_tensor(SS[:, 1, 0:40], SS[:, 0, 0:40], K[:, K_MH:K_MH + 40],
                                        ALU.pow).then_inc(hp, 1)
                for s in range(9, NPROJ):
                    item(l, s)
                for g in (1, 2):
                    rope_queries(nc.gpsimd, pool, l, g)
                for s in range(NPROJ, NPROJ + NOUT + 2):
                    item(l, s)
                norm_root(l * 2 + 1)
                s0 = NPROJ + NOUT + 2
                for s in range(s0, s0 + 4):
                    item(l, s)
                with pool.Fori(0, PAIRS - 1) as i:
                    for e in range(6):
                        s = s0 + 4 + e
                        low(l * NW + i * 6 + (s + 1), s % SPL, raw_of_split(s) % RAW, 1024)
            norm_root(2 * DEPTH)

        @block.scalar
        def _(act):
            def copy(dst, src):
                return nc.scalar.activation(dst, src, ACT.Copy)

            act.wait_ge(setup_v, 3)
            act.wait_ge(c_tr, 1)
            nc.scalar.activation(CT[:, :, 0:2], PS[:, 6, 0:16].rearrange("p (m k) -> p k m", m=2),
                                 ACT.Silu).then_inc(c_silu, 1)

            def split_hi(slot, raw, landed, used, width):
                act.wait_ge(raw_in[raw], landed)
                act.wait_ge(w_used, used)
                copy(W_hi[:, slot, 0:width], RW[:, raw, 0:width]).then_inc(w_hi, 1)

            def item(l, s):
                r = raw_of_split(s)
                split_hi(s % SPL, r % RAW, l * (16 * NRAW // RAW) + 16 * (r // RAW + 1),
                         l * NW + (s + 1), RMAX if s in (4, 5) else 1024)

            def square(N, t):
                if t >= 2:
                    act.wait_ge(ss_add, N * 7 + max(t - 2, 1))
                nc.scalar.activation(SQ[:, t % 2, :], X[:, t, :], ACT.Square).then_inc(sq_done, 1)

            def modulate(N, w, t):
                act.wait_ge(xn, N * KT + (t + 1))
                if t >= 2:
                    act.wait_ge(h_lo, N * KT + (t - 1))
                for cond, (c0, c1) in enumerate(((0, NLAT), (CTX0, CTX0 + NCTX))):
                    nc.scalar.activation(HF[:, t % 2, c0:c1], XN[:, t % 2, c0:c1], ACT.Identity,
                                         bias=MOD[:, 24 * w + t, cond:cond + 1],
                                         scale=AB[:, w, t, cond:cond + 1]).then_inc(hf, 1)
                act.wait_ge(hf, N * (2 * KT) + (2 * t + 2))
                copy(H_hi[:, t, :], HF[:, t % 2, :]).then_inc(h_hi, 1)

            def ada_move(l, ch, bank):
                act.wait_ge(ada_mm, l * (2 * NADA) + (2 * ch + 2))
                if ch > 0:
                    act.wait_ge(ada_sel, l * NADA + ch)
                copy(R[:, :], PS[:, bank, 0:256]).then_inc(ada_ev, 1)

            with act.Fori(0, DEPTH) as l:
                act.wait_ge(x_fin, l * KT + 1)
                for ch in range(ADA_A):
                    for t in ((0, 1, 2, 3), (4, 5), (6, 7))[ch] if ch < 3 else ():
                        act.wait_ge(x_fin, l * KT + (t + 1))
                        square(l * 2, t)
                    if ch == ADA_A - 1:
                        item(l, 0)
                    ada_move(l, ch, ch % 2)
                    if ch == 2:
                        act.wait_ge(v_tr, l + 1)
                        copy(VT[:, 0:70], PS[:, 3, 0:70])
                        copy(VT[0:96, 70:72], PS[0:96, 3, 70:72])
                        copy(VT[:, 72:204], PS[:, 3, 72:204]).then_inc(v_ev, 1)
                act.wait_ge(mod_ok, l * 4 + 2)
                for t in range(KT):
                    modulate(l * 2, 0, t)
                    if t == 1:
                        item(l, 1)

                for ch in range(len(TOKEN_CHUNKS)):
                    item(l, 2 * ch + 2)
                    act.wait_ge(w_used, l * NW + (SPL + 2 * ch + 2))
                    dst, c0, w = ((PMG, 0, 256), (PMG, 256, 256), (PMM, 0, 352), (PMS, 0, 256),
                                  (PMS, 256, 256))[ch]
                    for i in range(TT):
                        copy(dst[:, i, c0:c0 + w], PS[:, (TT * ch + i) % 8, 0:w]).then_inc(pj_ev, 1)
                    item(l, 2 * ch + 3)
                item(l, 12)
                act.wait_ge(w_used, l * NW + (SPL + 12))
                for o in range(2):
                    copy(GC[:, o, :].rearrange("p (h n) -> p h n", h=2),
                         PS[:, 2 + 2 * o:4 + 2 * o, 0:HALF]).then_inc(feat, 1)
                item(l, 13)
                item(l, 14)
                item(l, 15)

                act.wait_ge(head_in, l + 1)
                act.wait_ge(att_in, l * (16 * NATT) + 16 * NATT)
                act.wait_ge(zeroed, l * 3 + 3)
                for g, pm in enumerate((PMG, PMS)):
                    copy(KS[:, QT, 2 * g:2 * g + 2, 0:HD], pm[:, QT, 256:384].rearrange("p (h n) -> p h n", n=HD))
                    o = 160 + 2 * P * g
                    ins = copy(KS[:, PAST, 2 * g:2 * g + 2, HD:P],
                               CX[:, o:o + P].rearrange("p (h n) -> p h n", n=HD))
                ins.then_inc(raw_k, 1)

                def raw_queries(g):
                    if g < 2:
                        if g == 1:
                            act.wait_ge(tr_mm, l * NFILL + (FILL_AT[("Q", 3, 1)] + 1))
                        for t in range(TT):
                            src = (PMG, PMS)[g][:, t, 0:256].rearrange("p (h n) -> p h n", n=HD)
                            ins = copy(QS[:, t, :, HD:P] if t < QT else QS[:, t, :, 0:HD], src)
                        ins.then_inc(raw_q, 1)
                        return
                    all_moved(act, l, "MQ")
                    for t in range(TT):
                        src = PMG[:, t, 0:384].rearrange("p (h n) -> p h n", n=96)
                        copy(QS[:, t, :, 0:HD], src[:, :, 0:HD])
                        ins = copy(QS[:, t, :, 96:P] if t < QT else QS[:, t, :, HD:96], src[:, :, HD:96])
                    ins.then_inc(raw_q, 1)
                    kpe = PMM[:, QT, 320:352].rearrange("p (o n) -> p o n", o=1).to_broadcast([P, 4, ROPE])
                    copy(KS[:, QT, :, HD:96], kpe)
                    kpe = CX[:, 128:160].rearrange("p (o n) -> p o n", o=1).to_broadcast([P, 4, ROPE])
                    copy(KS[:, PAST, :, 96:P], kpe).then_inc(raw_k, 1)
                raw_queries(0)

                for o in range(2):
                    act.wait_ge(gated, l * 2 + (o + 1))
                    copy(H_hi[:, o, :], CV[:, o, :]).then_inc(ya_hi, 1)
                act.wait_ge(ya_lo, l * 2 + 2)

                def exponentials(h, q):
                    g, j = divmod(h, 4)
                    n = SIDX[(h, q)]
                    act.wait_ge(s_nb, l * NS_ + (n + 1))
                    if q == 0 and h >= 2:
                        act.wait_ge(tr_mm, l * NFILL + (FILL_AT[("P", h - 2, QT)] + 1))
                    nb = ST[:, 1, n % 4:n % 4 + 1]
                    if g == 1:
                        nc.scalar.activation(SE[:, n % 4:n % 4 + 1], SINK[:, j:j + 1], ACT.Exp,
                                             bias=nb).then_inc(s_sink, 1)
                    nc.scalar.activation(prob_ap(h, q), score_ap(h, q, n), ACT.Exp, bias=nb, scale=SCALES[g],
                                         accum_out=ST[:, 2, n % 4:n % 4 + 1]).then_inc(s_exp, 1)

                waiting = None
                for e in ORDER:
                    if e[0] == "S":
                        if waiting:
                            exponentials(*waiting)
                        waiting = e[1:]
                        continue
                    if e[0] == "T" and e[1][0] == "P" and waiting and waiting[0] == e[1][1]:
                        exponentials(*waiting)
                        waiting = None
                    if e[0] == "T" and by_scalar(e[1]):
                        evac_fill(act, copy, l, e[1])
                    elif e[0] == "PREP":
                        if e[1] == 2:
                            act.wait_ge(tr_mm, l * NFILL + (FILL_AT[("K", 3, 1)] + 1))
                        raw_queries(e[1])
                    elif e[0] == "MOVE":
                        ada_move(l, e[1], 7)
                    elif e == ("V", HEADS - 1, 0):
                        item(l, NPROJ)
                        item(l, NPROJ + 1)
                    elif e[0] == "V" and e[2] in (TT, QT):
                        h, k = e[1:]
                        i, r0, (c0, c1) = 6 * h + P_SEQ.index(k), HD * (h % 2), y_cols(k)
                        act.wait_ge(pv_mm, l * 6 * HEADS + (i + 1))
                        copy(H_hi[r0:r0 + HD, YTILE[h // 4] + h % 4 // 2, c0:c1],
                             PS[r0:r0 + HD, 6, 0:c1 - c0]).then_inc(y_hi, 1)
                    if waiting and (e[0] == "V" or e[0] == "MOVE"):
                        exponentials(*waiting)
                        waiting = None

                for ch in range(NOUT // 2):
                    item(l, NPROJ + 2 * ch + 2)
                    if ch < NOUT // 2 - 1:
                        item(l, NPROJ + 2 * ch + 3)
                    for t in range(2 * ch - 2, 2 * ch) if ch else ():
                        act.wait_ge(x_mid, l * KT + (t + 2))
                        square(l * 2 + 1, t)
                for t in (KT - 2, KT - 1):
                    act.wait_ge(x_mid, l * KT + (t + 2))
                    square(l * 2 + 1, t)
                item(l, NPROJ + NOUT + 1)
                for t in range(KT):
                    modulate(l * 2 + 1, 1, t)

                def up_out(i, e, used, first):
                    act.wait_ge(w_used, used)
                    if not first:
                        act.wait_ge(cv_done, l * 44 + i * 4 + (e + 1 - 4))
                    copy(U[:, e // 2, e % 2, 1:T + 1].rearrange("p (h n) -> p h n", h=2),
                         PS[:, 2 * e:2 * e + 2, 0:HALF]).then_inc(up_ev, 1)

                def silu(i, ch):
                    act.wait_ge(cv_done, l * 44 + i * 4 + (2 * ch + 2))
                    nc.scalar.activation(CF[:, ch, 0, :], CF[:, ch, 0, :], ACT.Silu).then_inc(silu_ok, 1)

                def g_high(i, ch, slot):
                    act.wait_ge(g_f, l * 22 + i * 2 + (ch + 1))
                    copy(G_hi[:, slot, ch, :], CF[:, ch, 1, :]).then_inc(g_hi, 1)

                s0 = NPROJ + NOUT
                for e in range(4):
                    up_out(0, e, l * NW + (SPL + s0 + e + 1), True)
                    item(l, s0 + e + 2)
                    if e == 1:
                        silu(0, 0)
                    if e == 2:
                        g_high(0, 0, 0)
                silu(0, 1)
                g_high(0, 1, 0)
                s0 += 4
                with act.Fori(0, PAIRS // 2) as m:
                    for b_ in range(2):
                        i = m * 2 + (1 + b_)

                        def item_i(e, b_=b_):
                            s = s0 + 6 * b_ + e
                            r = raw_of_split(s)
                            split_hi(s % SPL, r % RAW, l * (16 * NRAW // RAW) + m * 64 + 16 * (r // RAW + 1),
                                     l * NW + m * 12 + (s + 1), 1024)

                        def used_i(e, b_=b_):
                            return l * NW + m * 12 + (SPL + s0 + 6 * b_ + e + 1)
                        for e in range(4):
                            up_out(i, e, used_i(e), False)
                            item_i(e + 2)
                            if e == 1:
                                silu(i, 0)
                            if e == 2:
                                g_high(i, 0, (1 + b_) % 2)
                        silu(i, 1)
                        item_i(6)
                        g_high(i, 1, (1 + b_) % 2)
                        item_i(7)

            for t in range(KT):
                act.wait_ge(x_fin, DEPTH * KT + t + 1)
                square(2 * DEPTH, t)
            for t in range(KT):
                act.wait_ge(xn, 2 * DEPTH * KT + t + 1)
                for c0, c1 in ((0, NLAT), (CTX0, CTX0 + NCTX)):
                    ins = nc.scalar.activation(YO[:, t, c0:c1], XN[:, t % 2, c0:c1], ACT.Copy,
                                               scale=FN[:, t:t + 1])
                ins.then_inc(fin_y, 1)
            for i in range(TT):
                act.wait_ge(fin_tr, TT + i + 1)
                copy(OUT[:, i, 512:D], PS[:, i, :]).then_inc(fin_ev[1], 1)

        @block.tensor
        def _(pe):
            def mm(out, lhsT, rhs, start, stop):
                return nc.tensor.matmul(out, lhsT, rhs, start=start, stop=stop, skip_group_check=True)

            def tr(out, in_):
                n = in_.shape[0]
                return nc.tensor.transpose(out, in_, K[0:n, K_ID:K_ID + n])

            pe.wait_ge(const_in, 16)
            for i in range(TT):
                pe.wait_ge(x_in[i], 16)
                for hb in range(2):
                    n = 2 * i + hb
                    if n >= 6:
                        pe.wait_ge(x_ev, n - 5)
                    for t in range(4):
                        ins = tr(PS[:, n % 6, P * t:P * (t + 1)], XIN[:, i, P * (4 * hb + t):P * (4 * hb + t + 1)])
                    ins.then_inc(x_tr, 1)
            pe.wait_ge(c_in, 32)
            tr(PS[:, 6, 0:16], CR[:, :]).then_inc(c_tr, 1)
            pe.wait_ge(f_in, 16)
            tr(PS[:, 7, 0:KT], FR[:, :]).then_inc(f_tr, 1)
            pe.wait_ge(c_silu, 1)
            pe.wait_ge(f_ev, 1)
            pe.wait_ge(x_fin, KT)

            def ada_half(l, ch, kh, bank):
                a = 2 * ch + kh
                r = raw_of_ada(a)
                pe.wait_ge(raw_in[r % RAW], l * (16 * NRAW // RAW) + 16 * (r // RAW + 1))
                for kk in range(4):
                    ins = mm(PS[32 * kk:32 * kk + 32, bank, 0:256], CT[:, 4 * kh + kk, :],
                             RW[:, r % RAW, 256 * kk:256 * (kk + 1)], kh == 0, kh == 1)
                ins.then_inc(ada_mm, 1)

            def select(l, ch, bank, col):
                pe.wait_ge(ada_ev, l * NADA + (ch + 1))
                for o in range(2):
                    ins = mm(PS[:, bank, col + 2 * o:col + 2 * o + 2], R[:, P * o:P * (o + 1)],
                             K[:, K_SEL:K_SEL + 2], True, True)
                ins.then_inc(ada_sel, 1)

            def statistics(N):
                pe.wait_ge(ss_add, N * 7 + 7)
                for i in range(TT):
                    ins = mm(PS[:, 5, i:i + 1], SUM[:, TILE0[i]:TILE0[i] + P], ONES[:, 0:1], True, True)
                ins.then_inc(st_mm, 1)

            def spread_roots(N):
                for i in range(TT):
                    pe.wait_ge(dg, N * TT + (i + 1))
                    out = PS[:, 6, P * i:P * (i + 1)] if i < QT else PS[:, 7, 0:P]
                    ins = mm(out, ONES, DG[:, i, :], True, True)
                ins.then_inc(bc_mm, 1)

            def three(outs, w, cols, moving, first, last):
                mhi, mlo = moving
                for stat, mov, st, sp_ in ((W_hi, mhi, first, False), (W_hi, mlo, False, False),
                                           (W_lo, mhi, False, last)):
                    for hf_, out in enumerate(outs):
                        ins = mm(out, stat[:, w, cols:cols + P], mov[:, HALF * hf_:HALF * (hf_ + 1)], st, sp_)
                return ins

            def halves(pair):
                return [PS[:, 2 * pair + b_, 0:HALF] for b_ in range(2)]

            with pe.Fori(0, DEPTH) as l:
                pe.wait_ge(dn_add, l * (8 * PAIRS) + 8)
                for ch in range(ADA_A):
                    if ch >= 2:
                        pe.wait_ge(ada_ev, l * NADA + (ch - 1))
                    ada_half(l, ch, 0, ch % 2)
                    ada_half(l, ch, 1, ch % 2)
                    if ch:
                        select(l, ch - 1, 2, 4 * (ch - 1))
                    if ch == 2:
                        pe.wait_ge(vec_in, l * (16 * NVEC) + 16 * NVEC)
                        tr(PS[:, 3, 0:70], VR[:, :])
                        tr(PS[0:96, 3, 70:72], VQ[:, :])
                        tr(PS[:, 3, 72:138], VF[:, 0, :])
                        tr(PS[:, 3, 138:204], VF[:, 1, :]).then_inc(v_tr, 1)
                    if ch == 3:
                        statistics(l * 2)
                    if ch == 5:
                        spread_roots(l * 2)
                select(l, ADA_A - 1, 2, 4 * (ADA_A - 1))

                def w_ready(s):
                    pe.wait_ge(w_lo, l * NW + (RAW + s + 1))

                for ch, (_, w) in enumerate(TOKEN_CHUNKS):
                    for kh in range(2):
                        s = 2 * ch + kh
                        w_ready(s)
                        for kk in range(4):
                            k = 4 * kh + kk
                            if ch == 0:
                                pe.wait_ge(h_lo, l * (2 * KT) + (k + 1))
                            for i in range(TT):
                                idx = TT * ch + i
                                if k == 0 and idx >= 8:
                                    pe.wait_ge(pj_ev, l * 25 + (idx - 7))
                                out = PS[:, idx % 8, 0:w]
                                c0 = TILE0[i]
                                whi = W_hi[:, s % SPL, w * kk:w * (kk + 1)]
                                wlo = W_lo[:, s % SPL, w * kk:w * (kk + 1)]
                                mm(out, H_hi[:, k, c0:c0 + P], whi, k == 0, False)
                                mm(out, H_hi[:, k, c0:c0 + P], wlo, False, False)
                                ins = mm(out, H_lo[:, k, c0:c0 + P], whi, False, k == KT - 1)
                        ins.then_inc(w_used, 1)
                for f in range(3):
                    for kh in range(2):
                        s = 2 * len(TOKEN_CHUNKS) + 2 * f + kh
                        w_ready(s)
                        if kh == 0:
                            pe.wait_ge(pj_ev, l * 25 + (22 if f == 0 else 25))
                            if f == 2:
                                pe.wait_ge(feat, l * 2 + 2)
                        for kk in range(4):
                            for o in range(2):
                                pair = (1 + o, (3 + o) % 4, 1 + o)[f]
                                ins = three(halves(pair), s % SPL, 2 * P * kk + P * o,
                                            (H_hi[:, 4 * kh + kk, :], H_lo[:, 4 * kh + kk, :]),
                                            kh == 0 and kk == 0, kh == 1 and kk == 3)
                        ins.then_inc(w_used, 1)

                pe.wait_ge(gated, l * 2 + 2)
                pe.wait_ge(att_in, l * (16 * NATT) + 16 * NATT)
                for e in ORDER:
                    if e[0] == "T":
                        key = e[1]
                        n = FILL_AT[key]
                        bank = PS[:, 4 + n % 2, :]
                        if n >= 2:
                            pe.wait_ge(tr_ev[n % 2], l * NEV[n % 2] + n // 2)
                        if key[0] == "K":
                            _, kv, part = key
                            g = min(kv // 2, 2)
                            if part == 0 and kv == 4:
                                all_moved(pe, l, "MV")
                            if part == 0 and kv in (0, 4):
                                pe.wait_ge(raw_k, l * 2 + (1 if kv == 0 else 2))
                                pe.wait_ge(rot_k, l * 2 + (1 if kv == 0 else 2))
                                if kv == 0:
                                    pe.wait_ge(zeroed, l * 3 + 3)
                            for x, tile in enumerate((PAST, 0, 1, 2) if part == 0 else (3, 4)):
                                ins = tr(bank[:, P * x:P * (x + 1)], KS[:, tile, kv if kv < 4 else kv - 4, :])
                        elif key[0] == "Q":
                            _, h, part = key
                            if h % 4 == 0 and part == 0:
                                pe.wait_ge(raw_q, l * 3 + (h // 4 + 1))
                                pe.wait_ge(rot_q, l * 3 + (h // 4 + 1))
                            for x, tile in enumerate(range(QT) if part == 0 else (QT,)):
                                ins = tr(bank[:, P * x:P * (x + 1)], QS[:, tile, h % 4, :])
                        elif key[0] == "P":
                            _, h, k = key
                            if k == TT:
                                pe.wait_ge(s_norm, l * NS_ + NQ * (h + 1))
                                ins = tr(bank[:, 0:P], prob_ap(h, QT))
                            else:
                                q0, q1 = queries(h, k)
                                for q in range(q0, q1):
                                    c0 = q * (P + NLAT) + prob_col(h, q, k)
                                    ins = tr(bank[:, P * q:P * (q + 1)], PR[:, h % 2, c0:c0 + P])
                        elif key[0] == "MT":
                            i = key[1]
                            if i < TT:
                                tr(bank[0:96, 0:P], PMM[:, i, 0:96])
                                tr(bank[0:96, P:2 * P], PMM[:, i, 96:192])
                            ins = tr(bank[:, 2 * P:3 * P],
                                     PMM[:, i, 192:320] if i < TT else CX[:, 0:128])
                        elif key[0] == "MQ":
                            i = key[1]
                            m_ = FILL_AT[("MT", i)]
                            pe.wait_ge(tr_ev[m_ % 2], l * NEV[m_ % 2] + (m_ // 2 + 1))
                            pe.wait_ge(wq_ok, l + 1)
                            for k in range(2):
                                ins = mm(bank[:, 0:384], CQ[0:96, i % 2, k, :], WQ[:, k, :], k == 0, k == 1)
                        else:
                            i = key[1]
                            m_ = FILL_AT[("MT", i)]
                            pe.wait_ge(tr_ev[m_ % 2], l * NEV[m_ % 2] + (m_ // 2 + 1))
                            ins = mm(bank, CQ[:, i % 2, 2, :], WK[:, :], True, True)
                        ins.then_inc(tr_mm, 1)
                    elif e[0] == "S":
                        h, q = e[1:]
                        n, kv = SIDX[(h, q)], kv_of(h)
                        if n >= 2:
                            pe.wait_ge(s_exp, l * NS_ + (n - 1))
                        if q in (0, 1):
                            due = [("Q", h, 0), ("Q", h, 1), ("K", kv, 0), ("K", kv, 1)] if q == 0 else []
                            for key in due:
                                m_ = FILL_AT[key]
                                pe.wait_ge(tr_ev[m_ % 2], l * NEV[m_ % 2] + (m_ // 2 + 1))
                        b0 = 2 * (n % 2)
                        qt = QTR[:, h % 2, P * q:P * (q + 1)]
                        kt = KTR[:, kv % 2, :]
                        if q == QT:
                            ins = mm(PS[:, b0, 0:P], qt, kt[:, C_CTX:C_CTX + P], True, True)
                        elif h // 4 == 1:
                            lo, hi = window(h, q)
                            mm(PS[:, b0, 0:P], qt, kt[:, 0:P], True, True)
                            ins = mm(PS[:, b0, P:P * (1 + hi - lo)], qt,
                                     kt[:, C_LAT + P * lo:C_LAT + P * hi], True, False)
                            if q >= 1:
                                ins = mm(PS[:, b0, P:2 * P], IDENT, K[:, K_MASK:K_MASK + P], False, False)
                            if q <= QT - 2:
                                c0 = P * (hi - lo)
                                ins = mm(PS[:, b0, c0:c0 + P], IDENT, K[:, K_MASK + P:K_MASK + 2 * P],
                                         False, True)
                        else:
                            for b_ in range(2):
                                ins = mm(PS[:, b0 + b_, 0:HALFK], qt, kt[:, HALFK * b_:HALFK * (b_ + 1)],
                                         True, True)
                        ins.then_inc(s_mm, 1)
                    elif e[0] == "V":
                        h, k = e[1:]
                        i, r0 = 6 * h + P_SEQ.index(k), HD * (h % 2)
                        m_ = FILL_AT[("P", h, k)]
                        pe.wait_ge(tr_ev[m_ % 2], l * NEV[m_ % 2] + (m_ // 2 + 1))
                        yi = 2 * h + (k != TT)
                        if k in (TT, 0) and yi:
                            pe.wait_ge(y_lo, l * (2 * HEADS) + yi)
                        kv = kv_of(h) - 4 if h >= 8 else kv_of(h) % 2
                        tile = {TT: QT, 0: PAST}.get(k, k - 1)
                        c0, c1 = (0, P) if k == TT else (P * queries(h, k)[0], P * queries(h, k)[1])
                        if h == 8 and k == TT:
                            all_moved(pe, l, "MV")
                        mm(PS[r0:r0 + HD, 6, c0:c1], v_ap(h // 4, kv, tile), PT[:, i % 2, c0:c1],
                           k in (TT, 0), k in (TT, QT)).then_inc(pv_mm, 1)
                    elif e[0] == "ADA":
                        pe.wait_ge(ada_ev, l * NADA + e[1])
                        ada_half(l, e[1], 0, 7)
                        ada_half(l, e[1], 1, 7)
                    elif e[0] == "SEL":
                        select(l, e[1], 7, 256 + 4 * (e[1] - ADA_A))

                for ch in range(NOUT // 2):
                    for x in range(2):
                        s = NPROJ + 2 * ch + x
                        w_ready(s)
                        if x == 0:
                            if ch == 0:
                                pe.wait_ge(s_exp, l * NS_ + NS_)
                            elif ch == 1:
                                for b_ in range(2):
                                    pe.wait_ge(tr_ev[b_], l * NEV[b_] + NEV[b_])
                                pe.wait_ge(y_lo, l * (2 * HEADS) + 2 * HEADS)
                                pe.wait_ge(mod_ok, l * 4 + 4)
                            else:
                                pe.wait_ge(x_mid, l * KT + (1 + 2 * (ch - 1)))
                        if ch == 0:
                            pe.wait_ge(y_lo, l * (2 * HEADS) + (16 if x == 0 else 2 * HEADS))
                            pe.wait_ge(ya_lo, l * 2 + 2)
                        for kk in range(4):
                            k = 4 * (1 - x) + kk
                            for o in range(2):
                                ins = three(halves(2 * (ch % 2) + o), s % SPL, 2 * P * kk + P * o,
                                            (H_hi[:, k, :], H_lo[:, k, :]), x == 0 and kk == 0,
                                            x == 1 and kk == 3)
                        ins.then_inc(w_used, 1)
                pe.wait_ge(x_mid, l * KT + (1 + KT))
                statistics(l * 2 + 1)
                spread_roots(l * 2 + 1)

                def up_item(e, slot, ready, free, first):
                    pe.wait_ge(w_lo, ready)
                    free(e)
                    for k in range(KT):
                        if first and e == 0:
                            pe.wait_ge(h_lo, l * (2 * KT) + (KT + k + 1))
                        ins = three(halves(e), slot, P * k, (H_hi[:, k, :], H_lo[:, k, :]), k == 0, k == KT - 1)
                    ins.then_inc(w_used, 1)

                def down_item(q, slot, gslot, ready, free):
                    pe.wait_ge(w_lo, ready)
                    for t in range(4):
                        free(t)
                        for kc in range(2):
                            ins = three(halves(t), slot, 512 * kc + P * t,
                                        (G_hi[:, gslot, kc, :], G_lo[:, gslot, kc, :]), kc == 0, kc == 1)
                        if t < 3 and kc == 1:
                            ins.then_inc(dn_mm, 1)
                    ins.then_inc(w_used, 1)

                s0 = NPROJ + NOUT
                for e in range(4):
                    up_item(e, (s0 + e) % SPL, l * NW + (RAW + s0 + e + 1), lambda p: None, True)
                s0 += 4
                with pe.Fori(0, PAIRS // 2) as m:
                    for b_ in range(2):
                        i = m * 2 + (1 + b_)

                        def up_free(p):
                            pe.wait_ge(up_ev, l * 44 + i * 4 + (p + 1 - 4))
                            pe.wait_ge(dn_add, l * (8 * PAIRS) + i * 8 + (8 + 5 + p - 16))

                        def ready_i(e, b_=b_):
                            return l * NW + m * 12 + (RAW + s0 + 6 * b_ + e + 1)
                        for e in range(4):
                            up_item(e, (s0 + e) % SPL, ready_i(e), up_free, False)
                        pe.wait_ge(g_lo, l * 22 + i * 2)
                        down_item(0, s0 % SPL, b_ % 2, ready_i(4),
                                  lambda t: pe.wait_ge(up_ev, l * 44 + i * 4 + (t + 1)))
                        down_item(1, (s0 + 1) % SPL, b_ % 2, ready_i(5),
                                  lambda t: pe.wait_ge(dn_add, l * (8 * PAIRS) + i * 8 + (t + 1)))
                pe.wait_ge(g_lo, l * 22 + 22)
                for q in range(2):
                    s = NW - 2 + q
                    down_item(q, s % SPL, (PAIRS - 1) % 2, l * NW + (RAW + s + 1),
                              lambda t: pe.wait_ge(dn_add, l * (8 * PAIRS) + (8 + 8 * (PAIRS - 1) - 4 + 4 * q + t + 1)))

            pe.wait_ge(dn_add, 8 * PAIRS * DEPTH + 8)
            statistics(2 * DEPTH)
            spread_roots(2 * DEPTH)
            for n in range(2 * TT):
                hb, i = divmod(n, TT)
                if i == 0:
                    pe.wait_ge(fin_y, 4 * hb + 4)
                if hb:
                    pe.wait_ge(fin_ev[0], i + 1)
                for t in range(4):
                    ins = tr(PS[:, i, P * t:P * (t + 1)], YO[:, 4 * hb + t, TILE0[i]:TILE0[i] + P])
                ins.then_inc(fin_tr, 1)

        @block.vector
        def _(dve):
            v = nc.vector

            def copy(dst, src):
                return v.tensor_copy(dst, src)

            dve.wait_ge(const_in, 16)
            v.memset(CT[:, :, :], 0.0).then_inc(setup_v, 1)
            v.memset(X[:, :, NLAT:CTX0], 0.0).then_inc(setup_v, 1)
            v.memset(X[:, :, T - 2:T], 0.0).then_inc(setup_v, 1)
            for n in range(2 * TT):
                dve.wait_ge(x_tr, n + 1)
                c0, hb = TILE0[n // 2], n % 2
                ins = copy(X[:, 4 * hb:4 * hb + 4, c0:c0 + P], PS[:, n % 6, :].rearrange("p (t n) -> p t n", n=P))
                if n < 2 * TT - 1:
                    ins.then_inc(x_ev, 1)
                else:
                    ins.then_inc(x_fin, KT)
            dve.wait_ge(f_tr, 1)
            copy(FN[:, :], PS[:, 7, 0:KT]).then_inc(f_ev, 1)

            def add_square(N, t):
                dve.wait_ge(sq_done, N * KT + (t + 1))
                if t == 1:
                    v.tensor_tensor(SUM[:, :], SQ[:, 0, :], SQ[:, 1, :], ALU.add).then_inc(ss_add, 1)
                else:
                    dve.wait_ge(ss_add, N * 7 + (t - 1))
                    v.tensor_tensor(SUM[:, :], SUM[:, :], SQ[:, t % 2, :], ALU.add).then_inc(ss_add, 1)

            def norm_start(N):
                v.memset(HF[:, :, NLAT:CTX0], 0.0)
                v.memset(HF[:, :, T - 2:T], 0.0)
                dve.wait_ge(st_mm, N + 1)
                v.tensor_scalar(NS[:, 0, 0:TT], PS[:, 5, 0:TT], 1.0 / D, EPS, ALU.mult, ALU.add).then_inc(nv, 1)
                dve.wait_ge(rv, N + 1)
                for i in range(TT):
                    v.tensor_scalar(DG[:, i, :], IDENT, NS[:, 1, i:i + 1], None, ALU.mult).then_inc(dg, 1)
                for t in range(2):
                    normalise(N, t)

            def normalise(N, t):
                if t < 2:
                    dve.wait_ge(bc_mm, N + 1)
                elif isinstance(N, int):
                    dve.wait_ge(fin_y, t - 1)
                else:
                    dve.wait_ge(hf, N * (2 * KT) + (2 * t - 2))
                v.tensor_tensor(XN[:, t % 2, 0:NLAT], X[:, t, 0:NLAT], PS[:, 6, :], ALU.mult)
                v.tensor_tensor(XN[:, t % 2, CTX0:CTX0 + P], X[:, t, CTX0:CTX0 + P], PS[:, 7, 0:P],
                                ALU.mult).then_inc(xn, 1)

            def norm_rest(N):
                for t in range(KT):
                    dve.wait_ge(h_hi, N * KT + (t + 1))
                    v.tensor_tensor(H_lo[:, t, :], HF[:, t % 2, :], H_hi[:, t, :].bitcast(F32),
                                    ALU.subtract).then_inc(h_lo, 1)
                    if t + 2 < KT:
                        normalise(N, t + 2)

            def modulation(l, w):
                if w == 0:
                    t0, t1, src = 0, 16, PS[:, 2, 0:32]
                    dve.wait_ge(v_ev, l + 1)
                    dve.wait_ge(ada_sel, l * NADA + ADA_A)
                else:
                    t0, t1, src = 16, 48, PS[:, 7, 256:320]
                    dve.wait_ge(ada_sel, l * NADA + NADA)
                bias = VT[:, t0:t1].rearrange("p (t o) -> p t o", o=1).to_broadcast([P, t1 - t0, 2])
                v.tensor_tensor(MOD[:, t0:t1, :], src.rearrange("p (t o) -> p t o", o=2), bias,
                                ALU.add).then_inc(mod_ok, 1)
                dve.wait_ge(mod_ok, l * 4 + (2 * w + 1))
                gain = VT[:, 48 + KT * w:48 + KT * (w + 1)].rearrange("p (t o) -> p t o", o=1)
                s0 = 8 + 24 * w
                v.scalar_tensor_tensor(AB[:, w, :, :], MOD[:, s0:s0 + KT, :], 1.0,
                                       gain.to_broadcast([P, KT, 2]), ALU.add, ALU.mult).then_inc(mod_ok, 1)

            def residual(l, t):
                for cond, (c0, c1) in enumerate(((0, NLAT), (CTX0, CTX0 + NCTX))):
                    ins = v.scalar_tensor_tensor(X[:, t, c0:c1], DN[:, t, c0:c1],
                                                 MOD[:, 40 + t, cond:cond + 1], X[:, t, c0:c1],
                                                 ALU.mult, ALU.add)
                ins.then_inc(x_fin, 1)

            with dve.Fori(0, DEPTH) as l:
                own = Chain(dve, dve_own, l * DVE_OWN)
                for t in range(1, KT):
                    add_square(l * 2, t)
                norm_start(l * 2)
                v.memset(KS[:, 0:TT, :, HD:P], 0.0).then_inc(zeroed, 1)
                v.memset(KS[:, PAST, :, 0:HD], 0.0).then_inc(zeroed, 1)
                v.memset(QS[:, QT, :, HD:P], 0.0).then_inc(zeroed, 1)
                modulation(l, 0)
                norm_rest(l * 2)

                dve.wait_ge(pj_ev, l * 25 + 10)
                own.then(v.tensor_tensor(HS[:, :, :], PMG[:, :, 0:384], PMG[:, :, 0:384], ALU.mult))
                own.wait()
                r30 = SS[:, 0, 0:30].rearrange("p (t h) -> p t h", h=6)
                own.then(v.tensor_reduce(r30, HS[:, :, :].rearrange("p t (h n) -> p t h n", n=HD), AXX, ALU.add))
                own.wait()
                dve.wait_ge(pj_ev, l * 25 + 15)
                own.then(v.tensor_tensor(HS[:, :, 0:320], PMM[:, :, 0:320], PMM[:, :, 0:320], ALU.mult))
                own.wait()
                v.tensor_reduce(SS[:, 0, 30:35], HS[:, :, 0:192], AXX, ALU.add)
                own.then(v.tensor_reduce(SS[:, 0, 35:40], HS[:, :, 192:320], AXX, ALU.add))
                own.wait()
                for c0, c1, n in ((0, 30, HD), (30, 35, QLORA), (35, 40, KVLORA)):
                    ins = v.tensor_scalar(SS[:, 0, c0:c1], SS[:, 0, c0:c1], 1.0 / n, EPS, ALU.mult, ALU.add)
                ins.then_inc(hn, 1)
                dve.wait_ge(att_in, l * (16 * NATT) + 16 * NATT)
                v.tensor_scalar(SK[:, :], SINK[:, :], -1.0, None, ALU.mult)
                for k in range(2):
                    ins = v.tensor_scalar(WQ[:, k, :], WQ[:, k, :], VT[0:96, 70 + k:71 + k], None, ALU.mult)
                ins.then_inc(wq_ok, 1)
                dve.wait_ge(hp, l + 1)
                for t in range(TT):
                    r = SS[:, 1, 6 * t:6 * t + 6].rearrange("p (h o) -> p h o", o=1).to_broadcast([P, 6, HD])
                    qk = PMG[:, t, 0:384].rearrange("p (h n) -> p h n", n=HD)
                    ins = v.tensor_tensor(qk, qk, r, ALU.mult)
                    v.tensor_scalar(PMM[:, t, 0:192], PMM[:, t, 0:192], SS[:, 1, 30 + t:31 + t], None, ALU.mult)
                own.then(ins)
                own.wait()
                gain = GAIN[:, 0:384].rearrange("p (o n) -> p o n", o=1).to_broadcast([P, TT, 384])
                v.tensor_tensor(PMG[:, :, 0:384], PMG[:, :, 0:384], gain, ALU.mult)
                for t in range(TT):
                    ins = v.scalar_tensor_tensor(PMM[:, t, 192:320], PMM[:, t, 192:320], SS[:, 1, 35 + t:36 + t],
                                                 GAIN[:, 384:512], ALU.mult, ALU.mult)
                ins.then_inc(head_in, 1)
                dve.wait_ge(head_in, l + 1)
                dve.wait_ge(zeroed, l * 3 + 3)
                own.then(rope(v, own.wait, own.then, lambda t: PMM[:, t, 320:352].rearrange("p (h n) -> p h n", h=1),
                              lambda t: PMM[:, t, 320:352].rearrange("p (h n) -> p h n", h=1),
                              K_C32, K_S32, 1, ROPE))
                own.wait()
                dve.wait_ge(pj_ev, l * 25 + 25)
                for g, pm in enumerate((PMG, PMS)):
                    ins = rope(v, own.wait, own.then, lambda t: KS[:, t, 2 * g:2 * g + 2, 0:HD],
                               lambda t: pm[:, t, 256:384].rearrange("p (h n) -> p h n", n=HD),
                               K_C64, K_S64, 2, HD)
                    if g == 0:
                        own.then(ins)
                        own.wait()
                ins.then_inc(rot_k, 1)
                dve.wait_ge(rot_k, l * 2 + 1)
                rope(v, own.wait, own.then, lambda t: QS[:, t, :, 0:HD],
                     lambda t: PMG[:, t, 0:256].rearrange("p (h n) -> p h n", n=HD),
                     K_C64, K_S64, 4, HD).then_inc(rot_q, 1)

                v.memset(TP[:, :, 0:1], 0.0)
                v.memset(TP[:, :, T + 1:T + 2], 0.0)
                dve.wait_ge(w_used, l * NW + (SPL + 14))
                dve.wait_ge(feat, l * 2 + 2)
                for o in range(2):
                    pair = (3 + o) % 4
                    ins = v.tensor_tensor(TP[:, o, 1:T + 1].rearrange("p (h n) -> p h n", h=2),
                                          PS[:, 2 * pair:2 * pair + 2, 0:HALF],
                                          GC[:, o, :].rearrange("p (h n) -> p h n", h=2), ALU.mult)
                own.then(ins)
                own.wait()
                for o in range(2):
                    own.then(v.tensor_scalar(CV[:, o, :], TP[:, o, 0:T], VT[:, 64 + o:65 + o], None, ALU.mult))
                for tap in range(1, 3):
                    for o in range(2):
                        if o == 0:
                            own.wait()
                        own.then(v.scalar_tensor_tensor(CV[:, o, :], TP[:, o, tap:tap + T],
                                                        VT[:, 64 + 2 * tap + o:65 + 2 * tap + o], CV[:, o, :],
                                                        ALU.mult, ALU.add))
                own.wait()
                dve.wait_ge(w_used, l * NW + (SPL + 16))
                for o in range(2):
                    v.tensor_tensor(CV[:, o, :].rearrange("p (h n) -> p h n", h=2), PS[:, 2 + 2 * o:4 + 2 * o, 0:HALF],
                                    CV[:, o, :].rearrange("p (h n) -> p h n", h=2), ALU.mult).then_inc(gated, 1)
                for o in range(2):
                    dve.wait_ge(ya_hi, l * 2 + (o + 1))
                    v.tensor_tensor(H_lo[:, o, :], CV[:, o, :], H_hi[:, o, :].bitcast(F32),
                                    ALU.subtract).then_inc(ya_lo, 1)

                def maximum(h, q):
                    g, j = divmod(h, 4)
                    n = SIDX[(h, q)]
                    dve.wait_ge(s_mm, l * NS_ + (n + 1))
                    mx, nb = ST[:, 0, n % 4:n % 4 + 1], ST[:, 1, n % 4:n % 4 + 1]
                    s = score_ap(h, q, n)
                    v.tensor_reduce(mx, s, mybir.AxisListType.XY if len(s.shape) == 3 else AXX,
                                    ALU.max).then_inc(s_max, 1)
                    dve.wait_ge(s_max, l * NS_ + (n + 1))
                    if g == 1:
                        v.tensor_scalar(nb, mx, -SCALES[g], SK[:, j:j + 1], ALU.mult, ALU.min).then_inc(s_nb, 1)
                    else:
                        v.tensor_scalar(nb, mx, -SCALES[g], None, ALU.mult).then_inc(s_nb, 1)

                def normalise_probs(h, q):
                    n = SIDX[(h, q)]
                    dve.wait_ge(s_exp, l * NS_ + (n + 1))
                    den, rec = ST[:, 2, n % 4:n % 4 + 1], ST[:, 3, n % 4:n % 4 + 1]
                    if h // 4 == 1:
                        dve.wait_ge(s_sink, l * 20 + (n - 20 + 1))
                        v.tensor_tensor(den, den, SE[:, n % 4:n % 4 + 1], ALU.add).then_inc(s_den, 1)
                        dve.wait_ge(s_den, l * 20 + (n - 20 + 1))
                    v.reciprocal(rec, den).then_inc(s_rec, 1)
                    dve.wait_ge(s_rec, l * NS_ + (n + 1))
                    pr = prob_ap(h, q)
                    v.tensor_scalar(pr, pr, rec, None, ALU.mult).then_inc(s_norm, 1)

                waiting = None
                for e in ORDER:
                    if e[0] == "S":
                        maximum(*e[1:])
                        if waiting:
                            normalise_probs(*waiting)
                        waiting = e[1:]
                        continue
                    if e[0] == "T" and e[1][0] == "P" and waiting and waiting[0] == e[1][1]:
                        normalise_probs(*waiting)
                        waiting = None
                    if e[0] == "T" and not by_scalar(e[1]):
                        evac_fill(dve, copy, l, e[1])
                    elif e == ("PREP", 2):
                        dve.wait_ge(tr_mm, l * NFILL + (FILL_AT[("K", 3, 1)] + 1))
                        for t in range(QT):
                            copy(KS[:, t, :, HD:96],
                                 PMM[:, t, 320:352].rearrange("p (o n) -> p o n", o=1).to_broadcast([P, 4, ROPE]))
                        v.memset(KS[:, PAST, :, HD:96], 0.0).then_inc(rot_k, 1)
                    elif e[0] == "V" and e[2] in (TT, QT):
                        h, k = e[1:]
                        yi, r0, (c0, c1) = 2 * h + (k != TT), HD * (h % 2), y_cols(k)
                        tile = YTILE[h // 4] + h % 4 // 2
                        dve.wait_ge(y_hi, l * (2 * HEADS) + (yi + 1))
                        v.tensor_tensor(H_lo[r0:r0 + HD, tile, c0:c1], PS[r0:r0 + HD, 6, 0:c1 - c0],
                                        H_hi[r0:r0 + HD, tile, c0:c1].bitcast(F32), ALU.subtract).then_inc(y_lo, 1)
                modulation(l, 1)

                for t in range(KT):
                    if t % 2 == 0:
                        dve.wait_ge(w_used, l * NW + (SPL + NPROJ + t + 2))
                    b0 = 2 * (t % 4)
                    for cond, x0, bank, c0, c1 in ((0, 0, b0, 0, HALF), (0, HALF, b0 + 1, 0, NLAT - HALF),
                                                   (1, CTX0, b0 + 1, CTX0 - HALF, CTX0 + NCTX - HALF)):
                        x = X[:, t, x0:x0 + c1 - c0]
                        ins = v.scalar_tensor_tensor(x, PS[:, bank, c0:c1], MOD[:, 16 + t, cond:cond + 1], x,
                                                     ALU.mult, ALU.add)
                    ins.then_inc(x_mid, 1)
                    for x in {3: (1,), 5: (2, 3, 4, 5), 7: (6, 7)}.get(t, ()):
                        add_square(l * 2 + 1, x)
                norm_start(l * 2 + 1)
                norm_rest(l * 2 + 1)
                dve.wait_ge(new_out, l * 96 + 96)
                for t in range(KT):
                    ins = v.memset(DN[:, t, :], 0.0)
                own.then(ins)
                v.memset(U[:, :, :, 0:1], 0.0)
                own.then(v.memset(U[:, :, :, T + 1:T + 2], 0.0))
                own.wait()

                def convolve(i, ch, s, column, first):
                    dve.wait_ge(up_ev, l * 44 + i * 4 + (2 * ch + s + 1))
                    if not first:
                        dve.wait_ge(g_hi, l * 22 + i * 2 + (ch + 1 - 2))
                        dve.wait_ge(g_lo, l * 22 + i * 2 + (ch + 1 - 2))
                    x = 2 * (2 * ch + s)
                    v.tensor_scalar(CF[:, ch, s, :], U[:, ch, s, 0:T], column(0), None, ALU.mult).then_inc(cv_own, 1)
                    dve.wait_ge(cv_own, l * 88 + i * 8 + (x + 1))
                    v.scalar_tensor_tensor(CF[:, ch, s, :], U[:, ch, s, 1:T + 1], column(1), CF[:, ch, s, :],
                                           ALU.mult, ALU.add).then_inc(cv_own, 1)
                    dve.wait_ge(cv_own, l * 88 + i * 8 + (x + 2))
                    v.scalar_tensor_tensor(CF[:, ch, s, :], U[:, ch, s, 2:T + 2], column(2), CF[:, ch, s, :],
                                           ALU.mult, ALU.add).then_inc(cv_done, 1)

                def gate(i, ch):
                    dve.wait_ge(silu_ok, l * 22 + i * 2 + (ch + 1))
                    dve.wait_ge(cv_done, l * 44 + i * 4 + (2 * ch + 2))
                    v.tensor_tensor(CF[:, ch, 1, :], CF[:, ch, 1, :], CF[:, ch, 0, :], ALU.mult).then_inc(g_f, 1)

                def g_low(i, ch, slot):
                    dve.wait_ge(g_hi, l * 22 + i * 2 + (ch + 1))
                    v.tensor_tensor(G_lo[:, slot, ch, :], CF[:, ch, 1, :], G_hi[:, slot, ch, :].bitcast(F32),
                                    ALU.subtract).then_inc(g_lo, 1)

                def down_add(q, tiles, used, before):
                    for t in range(4):
                        if t < 3:
                            dve.wait_ge(dn_mm, tiles + (t + 1))
                        else:
                            dve.wait_ge(w_used, used)
                        if t == 0:
                            dve.wait_ge(dn_add, before)
                        out = DN[:, 4 * q + t, :].rearrange("p (h n) -> p h n", h=2)
                        v.tensor_tensor(out, PS[:, 2 * t:2 * t + 2, 0:HALF], out, ALU.add).then_inc(dn_add, 1)

                def column(tap, s, ch):
                    return VT[:, 72 + 44 * tap + 22 * s + ch:73 + 44 * tap + 22 * s + ch]
                convolve(0, 0, 0, lambda tap: column(tap, 0, 0), True)
                convolve(0, 0, 1, lambda tap: column(tap, 1, 0), True)
                convolve(0, 1, 0, lambda tap: column(tap, 0, 1), True)
                gate(0, 0)
                convolve(0, 1, 1, lambda tap: column(tap, 1, 1), True)
                g_low(0, 0, 0)
                gate(0, 1)
                g_low(0, 1, 0)
                s0 = NPROJ + NOUT + 4
                with dve.Fori(0, PAIRS // 2) as m:
                    for b_ in range(2):
                        i = m * 2 + (1 + b_)
                        def conv_i(ch, s, b_=b_):
                            convolve(i, ch, s, lambda tap: VT[:, bass.ds(
                                m * 4 + (72 + 44 * tap + 22 * s + 2 * (1 + b_) + ch), 1)], False)

                        def add_i(q):
                            down_add(q, l * (6 * PAIRS) + i * 6 + (3 * q - 6), l * NW + m * 12 + (SPL + s0 + 6 * b_ + 5 + q),
                                     l * (8 * PAIRS) + i * 8 + 4 * q)
                        conv_i(0, 0)
                        conv_i(0, 1)
                        conv_i(1, 0)
                        gate(i, 0)
                        conv_i(1, 1)
                        add_i(0)
                        g_low(i, 0, (1 + b_) % 2)
                        gate(i, 1)
                        add_i(1)
                        g_low(i, 1, (1 + b_) % 2)
                dve.wait_ge(cv_done, l * 44 + 44)
                dve.sem_inc(u_free, 1)
                for q in range(2):
                    down_add(q, l * (6 * PAIRS) + (6 * (PAIRS - 1) + 3 * q), l * NW + (SPL + NW - 1 + q),
                             l * (8 * PAIRS) + (8 * PAIRS + 4 * q))
                    for t in range(4 * q, 4 * q + 4):
                        dve.wait_ge(dn_add, l * (8 * PAIRS) + (8 * PAIRS + t + 1))
                        residual(l, t)
                assert own.n == DVE_OWN, own.n

            for t in range(1, KT):
                add_square(2 * DEPTH, t)
            norm_start(2 * DEPTH)
            for t in range(2, KT):
                normalise(2 * DEPTH, t)
            for i in range(TT):
                dve.wait_ge(fin_tr, i + 1)
                copy(OUT[:, i, 0:512], PS[:, i, :]).then_inc(fin_ev[0], 1)


_INS = ['x_prompt', 'x_sample', 'cache_mla_ckv', 'cache_mla_kpe', 'cache_gqa_k', 'cache_gqa_v', 'cache_swa_k',
        'cache_swa_v', 'c', 'c_ctx', 'w_ada', 'b_ada', 'norm1', 'w_in', 'conv_a', 'mla_q_norm', 'mla_wq_b',
        'mla_kv_norm', 'mla_wkv_b', 'gqa_q_norm', 'gqa_k_norm', 'swa_sink', 'w_out', 'norm2', 'w_up', 'conv_ff',
        'w_down', 'final_norm']
_OUTS = [((1, NCTX, D), 'float32'), ((1, NLAT, D), 'float32'), ((1, DEPTH, NCTX, KVLORA), 'float32'),
         ((1, DEPTH, NCTX, ROPE), 'float32')] + [((1, DEPTH, NCTX, 2, HD), 'float32')] * 4


def constants():
    k = np.zeros((P, K_N), np.float32)
    i, n = np.arange(P)[:, None], np.arange(P)[None, :]
    k[:, K_ID:K_ID + P] = i == n
    k[:, K_MASK:K_MASK + P] = np.where(n < i, NEG, 0)
    k[:, K_MASK + P:K_MASK + 2 * P] = np.where(n > i, NEG, 0)
    k[:, K_ONE:K_ONE + P] = 1
    for cond in range(2):
        k[np.arange(4) * 32 + cond, K_SEL + cond] = 1
    pos = np.arange(NLAT)
    for dim, kc, ks in ((HD, K_C64, K_S64), (ROPE, K_C32, K_S32)):
        half = dim // 2
        inv = np.power(np.float32(10000.0), -np.arange(0, half, 2, dtype=np.float32) / np.float32(half))
        row = (pos // GRID_W).astype(np.float32)[:, None] * inv
        col = (pos % GRID_W).astype(np.float32)[:, None] * inv
        cos = np.concatenate([np.cos(row)] * 2 + [np.cos(col)] * 2, axis=1)
        sin = np.concatenate([-np.sin(row), np.sin(row), -np.sin(col), np.sin(col)], axis=1)
        for t in range(QT):
            k[:, kc + dim * t:kc + dim * (t + 1)] = cos[P * t:P * (t + 1)]
            k[:, ks + dim * t:ks + dim * (t + 1)] = sin[P * t:P * (t + 1)]
    k[:, K_MH:K_MH + 40] = -0.5
    return k


def kernel(**inputs):
    import numpy as _np
    import concourse.bacc as _bacc
    from concourse import mybir as _mybir
    from concourse.bass_utils import run_bass_kernel_spmd as _run

    nc = _bacc.Bacc("TRN2", target_bir_lowering=False, num_devices=1)
    arrays, args = {}, []
    for name in _INS + ["consts"]:
        a = constants() if name == "consts" else _np.ascontiguousarray(inputs[name])
        arrays[f"in_{name}_dram"] = a
        args.append(nc.dram_tensor(f"in_{name}_dram", a.shape, _mybir.dt.from_np(a.dtype), kind="ExternalInput").ap())
    for i, (shape, dtype) in enumerate(_OUTS):
        dt = _mybir.dt.from_np(_np.dtype(dtype))
        args.append(nc.dram_tensor(f"out_{i}_dram", shape, dt, kind="ExternalOutput").ap())
    backbone_program(nc, *args)
    r = _run(nc, [arrays], core_ids=[0])
    return tuple(r.results[0][f"out_{i}_dram"] for i in range(len(_OUTS)))
```
